# Optimizing a Trainium2 kernel written in Bass

```python
import jax, jax.numpy as jnp
from jax import lax
import numpy as np

D_MODEL = 1024
BATCH = 1
SEQ = 512
DEPTH = 2
DEC_BATCH = 1
DEC_SEQ = 32
PAST_LEN = 1024

CHUNK = 64
Q_BLOCK = 128
D_PLE = 256
SB_HEADS = 8
SB_HEAD_DIM = 64
MLA_HEADS = 8
MLA_NOPE = 64
MLA_ROPE = 32
MLA_V = 64
KV_LORA = 128
D_FF = 2816
CONV_W = 3
ROPE_THETA = 10000.0
EPS = 1e-6

SB_W = SB_HEADS * SB_HEAD_DIM
MLA_QW = MLA_HEADS * (MLA_NOPE + MLA_ROPE)
MLA_OW = MLA_HEADS * MLA_V
IN_COLS = 3 * SB_W + MLA_QW + KV_LORA + MLA_ROPE + 2 * D_MODEL
SPLIT_POINTS = (SB_W, 2 * SB_W, 3 * SB_W, 3 * SB_W + MLA_QW, 3 * SB_W + MLA_QW + KV_LORA,
                3 * SB_W + MLA_QW + KV_LORA + MLA_ROPE, 3 * SB_W + MLA_QW + KV_LORA + MLA_ROPE + D_MODEL)
SB_SCALE = SB_HEAD_DIM ** -0.5
MLA_SCALE = (MLA_NOPE + MLA_ROPE) ** -0.5

kernel_name = 'stickbreak_mla_convffn_stream_step'

def rmsnorm(x, g):
    xf = x.astype(jnp.float32)
    y = xf * lax.rsqrt(jnp.mean(xf * xf, axis=-1, keepdims=True) + EPS)
    return (y * g.astype(jnp.float32)).astype(x.dtype)

def rope(x, pos):
    half = x.shape[-1] // 2
    freqs = jnp.power(ROPE_THETA, -jnp.arange(half, dtype=jnp.float32) / half)
    ang = pos.astype(jnp.float32)[:, None] * freqs[None, :]
    shape = (1, pos.shape[0]) + (1,) * (x.ndim - 3) + (half,)
    cos, sin = jnp.cos(ang).reshape(shape), jnp.sin(ang).reshape(shape)
    xf = x.astype(jnp.float32)
    x1, x2 = xf[..., :half], xf[..., half:]
    return jnp.concatenate([x1 * cos - x2 * sin, x1 * sin + x2 * cos], axis=-1).astype(x.dtype)

def sb_attend(q, k, v, q_pos, k_pos):
    z = jnp.einsum('bqhd,bkhd->bhqk', q, k).astype(jnp.float32) * SB_SCALE
    visible = k_pos[None, :] < q_pos[:, None]
    log_1mb = jnp.where(visible, jax.nn.log_sigmoid(-z), 0.0)
    suffix = lax.cumsum(log_1mb, axis=3, reverse=True) - log_1mb
    a = jnp.where(visible, jnp.exp(jax.nn.log_sigmoid(z) + suffix), 0.0)
    return jnp.einsum('bhqk,bkhd->bqhd', a.astype(v.dtype), v)

def mla_attend(q_lat, q_rope, c_kv, k_rope, q_pos, k_pos):
    s = (jnp.einsum('bqhl,bkl->bhqk', q_lat, c_kv).astype(jnp.float32)
         + jnp.einsum('bqhr,bkr->bhqk', q_rope, k_rope).astype(jnp.float32)) * MLA_SCALE
    visible = (k_pos[None, :] // CHUNK) <= (q_pos[:, None] // CHUNK)
    p = jax.nn.softmax(jnp.where(visible, s, -jnp.inf), axis=-1)
    return jnp.einsum('bhqk,bkl->bqhl', p.astype(c_kv.dtype), c_kv)

def sweep_query_blocks(fn, qs, q_pos):
    B, S = qs[0].shape[:2]
    nb = S // Q_BLOCK
    def to_blocks(a):
        return jnp.moveaxis(a.reshape((B, nb, Q_BLOCK) + a.shape[2:]), 1, 0)
    out = lax.map(lambda args: fn(args[0], args[1]),
                  (tuple(to_blocks(a) for a in qs), q_pos.reshape(nb, Q_BLOCK)))
    out = jnp.moveaxis(out, 0, 1)
    return out.reshape((B, S) + out.shape[3:])

def trunk_layer(x, p, pos, past, lw):
    (w_in, ckv_gain, w_uk, w_uv, w_proj_sb, w_proj_mla, w_out, g_pre_mix, g_post_mix,
     g_pre_ffn, g_post_ffn, w_up, conv_w, conv_b, w_down, w_ple_gate, w_ple_proj) = lw
    B, T, _ = x.shape
    h = rmsnorm(x, g_pre_mix)
    q_sb, k_sb, v_sb, q_mla, ckv, k_rope, gate_a, gate_b = jnp.split(h @ w_in, SPLIT_POINTS, axis=-1)
    q_sb = q_sb.reshape(B, T, SB_HEADS, SB_HEAD_DIM)
    k_sb = k_sb.reshape(B, T, SB_HEADS, SB_HEAD_DIM)
    v_sb = v_sb.reshape(B, T, SB_HEADS, SB_HEAD_DIM)
    q_mla = q_mla.reshape(B, T, MLA_HEADS, MLA_NOPE + MLA_ROPE)
    q_nope, q_rope = q_mla[..., :MLA_NOPE], rope(q_mla[..., MLA_NOPE:], pos)
    ckv = rmsnorm(ckv, ckv_gain)
    k_rope = rope(k_rope, pos)
    q_lat = jnp.einsum('bthn,lhn->bthl', q_nope, w_uk)
    if past is None:
        k_pos = pos
        conv_past = jnp.zeros((B, CONV_W - 1, 2 * D_FF), x.dtype)
        o_sb = sweep_query_blocks(lambda qs, qp: sb_attend(qs[0], k_sb, v_sb, qp, k_pos), (q_sb,), pos)
        o_lat = sweep_query_blocks(lambda qs, qp: mla_attend(qs[0], qs[1], ckv, k_rope, qp, k_pos),
                                   (q_lat, q_rope), pos)
    else:
        pk, pv, pc, pr, conv_past = past
        k_all = jnp.concatenate([pk, k_sb], axis=1)
        v_all = jnp.concatenate([pv, v_sb], axis=1)
        c_all = jnp.concatenate([pc, ckv], axis=1)
        r_all = jnp.concatenate([pr, k_rope], axis=1)
        k_pos = jnp.arange(pk.shape[1] + T, dtype=jnp.int32)
        o_sb = sb_attend(q_sb, k_all, v_all, pos, k_pos)
        o_lat = mla_attend(q_lat, q_rope, c_all, r_all, pos, k_pos)
    o_mla = jnp.einsum('bthl,lhv->bthv', o_lat, w_uv)
    y_a = o_sb.reshape(B, T, SB_W) @ w_proj_sb
    y_b = o_mla.reshape(B, T, MLA_OW) @ w_proj_mla
    mix = (jax.nn.sigmoid(gate_a) * y_a + jax.nn.sigmoid(gate_b) * y_b) @ w_out
    x = x + rmsnorm(mix, g_post_mix)
    u = rmsnorm(x, g_pre_ffn) @ w_up
    u_ext = jnp.concatenate([conv_past, u], axis=1)
    uc = conv_b
    for i in range(CONV_W):
        uc = uc + u_ext[:, i:i + T] * conv_w[i]
    gate, val = uc[..., :D_FF], uc[..., D_FF:]
    f = (jax.nn.gelu(gate, approximate=True) * val) @ w_down
    x = x + rmsnorm(f, g_post_ffn)
    x = x + jax.nn.sigmoid(x @ w_ple_gate) * (p @ w_ple_proj)
    new_conv = u_ext[:, -(CONV_W - 1):]
    return x, (k_sb, v_sb, ckv, k_rope, new_conv)

def setup_inputs(seed: int = 0) -> dict:
    key = jax.random.key(seed)
    ks = jax.random.split(key, 32)
    def nrm(k, shape, scale=1.0):
        return jax.random.normal(k, shape, jnp.float32) * scale
    def gain(k, n):
        return 1.0 + 0.01 * jax.random.normal(k, (DEPTH, n), jnp.float32)
    return {
        'x_prompt': nrm(ks[0], (BATCH, SEQ, D_MODEL)),
        'x_sample': nrm(ks[1], (DEC_BATCH, DEC_SEQ, D_MODEL)),
        'p_prompt': nrm(ks[2], (DEPTH, BATCH, SEQ, D_PLE)),
        'p_sample': nrm(ks[3], (DEPTH, DEC_BATCH, DEC_SEQ, D_PLE)),
        'cache_sb_k': nrm(ks[4], (DEPTH, DEC_BATCH, PAST_LEN, SB_HEADS, SB_HEAD_DIM)),
        'cache_sb_v': nrm(ks[5], (DEPTH, DEC_BATCH, PAST_LEN, SB_HEADS, SB_HEAD_DIM)),
        'cache_mla_ckv': nrm(ks[6], (DEPTH, DEC_BATCH, PAST_LEN, KV_LORA)),
        'cache_mla_krope': nrm(ks[7], (DEPTH, DEC_BATCH, PAST_LEN, MLA_ROPE)),
        'state_ffn_conv': nrm(ks[8], (DEPTH, DEC_BATCH, CONV_W - 1, 2 * D_FF)),
        'w_in': nrm(ks[9], (DEPTH, D_MODEL, IN_COLS), D_MODEL ** -0.5),
        'ckv_gain': gain(ks[10], KV_LORA),
        'w_uk': nrm(ks[11], (DEPTH, KV_LORA, MLA_HEADS, MLA_NOPE), KV_LORA ** -0.5),
        'w_uv': nrm(ks[12], (DEPTH, KV_LORA, MLA_HEADS, MLA_V), KV_LORA ** -0.5),
        'w_proj_sb': nrm(ks[13], (DEPTH, SB_W, D_MODEL), SB_W ** -0.5),
        'w_proj_mla': nrm(ks[14], (DEPTH, MLA_OW, D_MODEL), MLA_OW ** -0.5),
        'w_out': nrm(ks[15], (DEPTH, D_MODEL, D_MODEL), D_MODEL ** -0.5),
        'g_pre_mix': gain(ks[16], D_MODEL),
        'g_post_mix': gain(ks[17], D_MODEL),
        'g_pre_ffn': gain(ks[18], D_MODEL),
        'g_post_ffn': gain(ks[19], D_MODEL),
        'w_up': nrm(ks[20], (DEPTH, D_MODEL, 2 * D_FF), D_MODEL ** -0.5),
        'conv_w': nrm(ks[21], (DEPTH, CONV_W, 2 * D_FF), CONV_W ** -0.5),
        'conv_b': nrm(ks[22], (DEPTH, 2 * D_FF), 0.01),
        'w_down': nrm(ks[23], (DEPTH, D_FF, D_MODEL), D_FF ** -0.5),
        'w_ple_gate': nrm(ks[24], (DEPTH, D_MODEL, D_MODEL), D_MODEL ** -0.5),
        'w_ple_proj': nrm(ks[25], (DEPTH, D_PLE, D_MODEL), D_PLE ** -0.5),
    }

def reference(x_prompt, x_sample, p_prompt, p_sample, cache_sb_k, cache_sb_v, cache_mla_ckv,
              cache_mla_krope, state_ffn_conv, w_in, ckv_gain, w_uk, w_uv, w_proj_sb, w_proj_mla,
              w_out, g_pre_mix, g_post_mix, g_pre_ffn, g_post_ffn, w_up, conv_w, conv_b, w_down,
              w_ple_gate, w_ple_proj):
    T_p = x_prompt.shape[1]
    T_s = x_sample.shape[1]
    past_len = cache_sb_k.shape[2]
    pos_p = jnp.arange(T_p, dtype=jnp.int32)
    pos_s = past_len + jnp.arange(T_s, dtype=jnp.int32)
    xp, xs = x_prompt, x_sample
    st_p, st_s = [], []
    for i in range(DEPTH):
        lw = (w_in[i], ckv_gain[i], w_uk[i], w_uv[i], w_proj_sb[i], w_proj_mla[i], w_out[i],
              g_pre_mix[i], g_post_mix[i], g_pre_ffn[i], g_post_ffn[i], w_up[i], conv_w[i],
              conv_b[i], w_down[i], w_ple_gate[i], w_ple_proj[i])
        xp, sp = trunk_layer(xp, p_prompt[i], pos_p, None, lw)
        past = (cache_sb_k[i], cache_sb_v[i], cache_mla_ckv[i], cache_mla_krope[i], state_ffn_conv[i])
        xs, ss = trunk_layer(xs, p_sample[i], pos_s, past, lw)
        st_p.append(sp)
        st_s.append(ss)
    sbk_p = jnp.stack([s[0] for s in st_p])
    sbv_p = jnp.stack([s[1] for s in st_p])
    ckv_p = jnp.stack([s[2] for s in st_p])
    kr_p = jnp.stack([s[3] for s in st_p])
    conv_p = jnp.stack([s[4] for s in st_p])
    sbk_s = jnp.stack([s[0] for s in st_s])
    sbv_s = jnp.stack([s[1] for s in st_s])
    ckv_s = jnp.stack([s[2] for s in st_s])
    kr_s = jnp.stack([s[3] for s in st_s])
    conv_s = jnp.stack([s[4] for s in st_s])
    return (xp, xs, sbk_p, sbv_p, ckv_p, kr_p, conv_p, sbk_s, sbv_s, ckv_s, kr_s, conv_s)


_drawn_inputs = setup_inputs


def setup_inputs(seed=0):
    import zlib

    import numpy as np

    out = dict(_drawn_inputs(seed))
    spreads = {}
    factors = {'ckv_gain': 5.378,
     'g_pre_mix': 4.326,
     'g_post_mix': 5.427,
     'g_pre_ffn': 4.95,
     'g_post_ffn': 7.569,
     'conv_b': 5.256,
     'cache_mla_ckv': 3.387,
     'cache_mla_krope': 3.044}
    for name, (base, spread) in spreads.items():
        noise = np.random.default_rng([zlib.crc32(name.encode()), seed]).standard_normal(out[name].shape)
        drawn = base * np.exp(spread * noise) if base else spread * noise
        out[name] = __import__('jax').numpy.asarray(drawn.astype(out[name].dtype))
    for name, factor in factors.items():
        out[name] = (out[name] * factor).astype(out[name].dtype)
    return out
```

```python
from contextlib import ExitStack

import concourse.bass as bass
import numpy as np
from concourse import mybir

F32 = mybir.dt.float32
F32R = mybir.dt.float32r
BF16 = mybir.dt.bfloat16
ALU = mybir.AluOpType
ACT = mybir.ActivationFunctionType

P = 128
DEPTH = 2
D = 1024
KT = D // P
SEQ, DEC, PAST = 512, 32, 1024
T = SEQ + DEC
HT = T // 2
QB = SEQ // P
CB = PAST // P
TAIL = T - P
SH, SD = 8, 64
MH, NOPE, ROPE, MV, LORA = 8, 64, 32, 64, 128
CHUNK = 64
DFF = 2816
FT = DFF // P
PLE = 256
EPS = 1e-6
SB_SCALE = SD ** -0.5
MLA_SCALE = (NOPE + ROPE) ** -0.5
NEG = -1e30
PAIRS = SH // 2
CW = KT * P
FFN_PARTS = [8, 8, 6]
RAW_SLOTS, W_SLOTS = 2, 3
RW = 24448

CHUNKS = [("v", i) for i in range(4)]
for _t in range(PAIRS):
    CHUNKS += [("q", _t), ("k", _t)]
CHUNKS += [("c", 0), ("kr", 0), ("qr", 0), ("qr", 1), ("ukuv", 0)]
CHUNKS += [("qn", t) for t in range(PAIRS)]
for _j in range(KT):
    CHUNKS += [("ga", _j), ("gb", _j), ("proj", _j)]
CHUNKS += [("out", j) for j in range(KT)]
_F0 = [sum(FFN_PARTS[:i]) for i in range(len(FFN_PARTS) + 1)]


def _up(i):
    return [c for j in range(_F0[i], _F0[i + 1]) for c in (("upg", j), ("upv", j))]


def _down(i):
    return [("down", i, j) for j in range(KT)]


CHUNKS += _up(0) + _up(1) + _down(0) + _up(2) + _down(1) + _down(2)
CHUNKS += [c for j in range(KT) for c in (("pleg", j), ("plep", j))]
CHUNK_AT = {c: n for n, c in enumerate(CHUNKS)}
RING = [c for c in CHUNKS if c[0] != "ukuv"]
RING_AT = {c: n for n, c in enumerate(RING)}


def chunk_floats(c):
    if c[0] == "down":
        return FFN_PARTS[c[1]] * P
    return PLE // P * P if c[0] == "plep" else CW


V_GPM, V_GQM, V_GPF, V_GQF = 0, KT, 2 * KT, 3 * KT
V_CW = 4 * KT
V_CB = V_CW + 3 * 2 * FT
V_CG = V_CB + 2 * FT
V_ST = V_CG + 1
NV = V_ST + 2 * 2 * FT + 1

C_ONES, C_ID, C_TRI, C_NEG1 = 0, P, 2 * P, 3 * P
C_MD, C_MS, C_MM, C_MT = 4 * P, 5 * P, 7 * P, 8 * P
NCONST = 9 * P


def _q_swap(n=32):
    return [(i + n // 2) % n for i in range(n)]


def build(nc, x_in, p_in, wstream, vec, kc, vc, cct, cc, krc, consts, trig,
          y_out, k_out, v_out, c_out, kr_out, conv_out):
    top = ExitStack()
    with top:
        def sb(name, shape, dt=F32, stack=top):
            return stack.enter_context(nc.sbuf_tensor(name, shape, dt))

        ps = top.enter_context(nc.psum_tensor("ps", [P, 8, 512], F32))
        xT = sb("xT", [P, KT, T])
        con = sb("con", [P, NCONST - 2 * P])
        ones = con[:, C_ONES:C_ONES + P]
        ident = con[:, C_ID:C_ID + P]
        exact = sb("exact", [P, 2, P], F32R)
        masks = sb("masks", [P, 6, P], BF16)
        epsb = sb("epsb", [P, 1])
        ident_b = masks[:, 0]

        raw = sb("raw", [P, RAW_SLOTS, CW])
        wsp = sb("wsp", [P, W_SLOTS, 2, CW], F32R)
        xn = sb("xn", [P, 2, KT, T], F32R)
        R = sb("R", [P, RW], F32R)
        A = sb("A", [P, KT * T])
        mix = sb("mix", [P, 6, T + 4])
        rstd = sb("rstd", [P, T])
        acc = sb("acc", [P, T])
        vv = sb("vv", [P, NV])
        small = sb("small", [P, 8])
        ctail = sb("ctail", [P, 2 * FT, 4])

        fT = A[:, :].rearrange("p (k t) -> p k t", t=T)

        def reg(off, *dims):
            n = int(np.prod(dims))
            assert off + n <= RW, (off, n)
            ap = R[:, off:off + n]
            if len(dims) == 1:
                return ap
            names = "abcd"[:len(dims)]
            s = {names[i]: dims[i] for i in range(1, len(dims))}
            return ap.rearrange(f"p ({' '.join(names)}) -> p {' '.join(names)}", **s)

        o_sb = reg(0, 2, PAIRS, T)
        b = 2 * PAIRS * T
        v_s = reg(b, 2, QB + 1, SH * SD)
        b1 = b + 2 * (QB + 1) * SH * SD
        qk = reg(b1, 2, 2, 2, T)
        kcs = reg(b1, 2, 4, PAIRS * P)
        b2 = b1 + 8 * T
        SPW = sum(SEQ - kb * P for kb in range(QB))
        sp = reg(b2, 2, 2 * SPW)
        b3 = b2 + 4 * SPW
        att = reg(b3, 2, 2, 512)
        b4 = b3 + 2048
        k_tail = reg(b4, 2, PAIRS, P)
        q_smp = reg(b4 + 2 * PAIRS * P, 2, PAIRS, 2 * DEC)
        o_ml = reg(b, 2, PAIRS, T)
        m0 = b + 2 * PAIRS * T
        cT = reg(m0, 2, T)
        ctok = reg(m0 + 2 * T, 2, QB + 1, P)
        m1 = m0 + 2 * T + 2 * (QB + 1) * P
        krT = reg(m1, 2, T)
        ukuv = reg(m1 + 2 * T, 2, CW)
        m2 = m1 + 2 * T + 2 * CW
        ql_smp = reg(m2, 2, MH, DEC)
        qr_smp = reg(m2 + 2 * MH * DEC, 2, 2, P)
        m3 = m2 + 2 * MH * DEC + 4 * P
        qr = reg(m3, 2, 2, T)
        qn = reg(m3 + 4 * T, 2, T)
        ql = reg(m3 + 6 * T, 2, SEQ)
        m4 = m3 + 6 * T + 2 * SEQ
        PTS = 384
        PTW = 3 * PTS + 512
        pT = reg(m4, 2, PTW)
        ol = reg(m4 + 2 * PTW, 2, SEQ)
        cache_s = reg(m3, 2, 2, PAST)
        pT_s = reg(m3 + 4 * PAST, 2, CB + 1, 2 * P)
        ol_s = reg(m3 + 4 * PAST + 4 * (CB + 1) * P, 2, 2 * P)
        mixin = reg(b + 2 * PAIRS * T, 2, KT, T)
        g_s = [reg(0, 2, 8, T), reg(16 * T, 2, 8, T)]
        p_s = reg(32 * T, 2, 2, T)

        tsp = A[:, 0:1024].rearrange("p (s n) -> p s n", n=512)
        araw = A[:, 1024:2048].rearrange("p (s n) -> p s n", n=512)
        kraw = A[:, 2048:2048 + T]
        vraw = A[:, 2592:2592 + 1024].rearrange("p (s n) -> p s n", n=512)
        kcraw = [vraw[:, 0], vraw[:, 1]]
        vcraw = [A[:, 2048:2560], A[:, 3616:4128]]
        craw = A[:, 0:T]
        rope = [A[:, T:2 * T], A[:, 2 * T:3 * T]]
        prw = A[:, 3 * T:3 * T + 1024].rearrange("p (s n) -> p s n", n=512)
        craws = A[:, 0:2 * PAST].rearrange("p (k n) -> p k n", n=PAST)
        psm = A[:, 2 * PAST:2 * PAST + (CB + 1) * P]
        rsum, negmax = small[:, 0:2], small[:, 2:4]
        cos, sin = mix[:, 0, 0:T], mix[:, 1, 0:T]
        sq = [mix[:, 2, 0:T], mix[:, 3, 0:T]]
        tmp = [mix[:, 4, 0:T], mix[:, 5, 0:T]]
        EXT = T + 4
        uext = [mix[:, 0], mix[:, 1]]
        uc = [mix[:, 2, 0:T + 2], mix[:, 3, 0:T + 2]]
        gel = mix[:, 4, 0:T + 2]
        gt = mix[:, 5, 0:T]

        def halves(ap):
            return ap.rearrange("p (h n) -> p h n", h=2)

        def ptile(n):
            return ps[:, 2 * (n % 2):2 * (n % 2) + 2, 0:HT]

        ZB, OB = 4, 7
        s_view = ps[:, ZB:ZB + 3].rearrange("p b n -> p (b n)")[:, 0:(CB + 1) * P]

        def pt_view(x, qb):
            o = m4 + x * PTW + qb * P
            return R[:, o:o + PTS * (qb + 1)].rearrange("p (b q) -> p b q", q=PTS)[:, :, 0:P]

        with ExitStack() as st:
            pre = {n: st.enter_context(nc.semaphore(n)) for n in ("con_in", "x_in", "made")}
            late = sb("late", [P, 2 * P])
            block = st.enter_context(nc.Block())

            @block.sync
            def _(sp_):
                sp_.dma_start(con[:], consts[:, 0:NCONST - 2 * P]).then_inc(pre["con_in"], 16)
                sp_.dma_start(late[:], consts[:, NCONST - 2 * P:]).then_inc(pre["con_in"], 16)
                sp_.dma_start(xT[:], x_in.rearrange("(k p) t -> p k t", p=P)).then_inc(pre["x_in"], 16)
                sp_.wait_ge(pre["x_in"], 16)

            @block.vector
            def _(dve):
                dve.wait_ge(pre["con_in"], 32)
                nc.vector.tensor_copy(exact[:, 0], con[:, C_TRI:C_TRI + P]).then_inc(pre["made"], 1)
                nc.vector.tensor_copy(exact[:, 1], con[:, C_NEG1:C_NEG1 + P]).then_inc(pre["made"], 1)
                nc.vector.tensor_copy(masks[:, 0], ident).then_inc(pre["made"], 1)
                nc.vector.tensor_copy(masks[:, 1:4].rearrange("p a b -> p (a b)"), con[:, C_MD:C_MD + 3 * P]).then_inc(pre["made"], 1)
                nc.vector.tensor_copy(masks[:, 4:6].rearrange("p a b -> p (a b)"), late[:]).then_inc(pre["made"], 1)
                nc.vector.memset(epsb[:], EPS).then_inc(pre["made"], 1)
                dve.wait_ge(pre["made"], 6)

        m_units = [(h, qb) for h in range(MH) for qb in range(QB)]
        NM = len(m_units)
        M_STEPS = NM + 4

        def m_tiles(s):
            out = []
            if s == 0 or (s + 2) % (2 * QB) == 0 and s + 2 < NM:
                out.append(("qn", (s + 2) // (2 * QB)))
            if s % QB == 0 and s < NM:
                out.append(("ql", s // QB))
            if s >= QB + 3 and (s - 4) % QB == QB - 1:
                out.append(("uv", (s - 4) // QB))
            return out

        PT = [("nm", 0), ("q", 0), ("k", 0)]
        for t in range(1, PAIRS):
            PT += [("q", t), ("k", t)]
        PT += [("c", 0), ("kr", 0), ("qr", 0), ("qr", 1), ("cn", 0), ("ct", 0)]
        for s in range(M_STEPS):
            PT += m_tiles(s)
        PT += [("uvs", 0)]
        for j in range(KT):
            PT += [("ga", j), ("gb", j), ("ya", j), ("yb", j)]
        PT += [("out", j) for j in range(KT)] + [("nm", 1), ("nm", 2)]
        PT += _up(0) + _up(1) + _down(0) + _up(2) + _down(1) + _down(2) + [("nm", 3)]
        for j in range(KT):
            PT += [("pleg", j), ("plep", j)]
        AT = {t: n for n, t in enumerate(PT)}
        assert len(AT) == len(PT)
        ACT_ONLY = {"c", "kr", "qr", "cn", "nm", "ga", "gb", "out", "upg", "upv", "pleg"}

        def readers(t):
            if t[0] in ("ya", "yb", "plep") or (t[0] == "down" and t[1] > 0):
                return 0, 1
            return (1, 0) if t[0] in ACT_ONLY or t[0] == "down" else (1, 1)

        act_upto, dve_upto = [0], [0]
        for t in PT:
            act_upto.append(act_upto[-1] + readers(t)[0])
            dve_upto.append(dve_upto[-1] + readers(t)[1])

        def aread(t):
            return act_upto[AT[t] + 1]

        def dread(t):
            return dve_upto[AT[t] + 1]

        def last_tile(c):
            if c[0] == "proj":
                return ("yb", c[1])
            return c

        units = [("p", h, kb) for h in range(SH) for kb in reversed(range(QB))]
        units += [("s", 0, kb) for kb in reversed(range(CB + 1))]
        NU, NPU = len(units), SH * QB
        FIRST_CACHE = NPU + 1
        fill = {}
        for t in range(1, PAIRS):
            fill[(t - 1) * 2 * QB + 2] = ("q", t)
            fill[(t - 1) * 2 * QB + 5] = ("k", t)
        LAG_CUM, LAG_PV = 2, 3
        NSTEP = NU + LAG_PV + 1

        def width(u):
            return SEQ - P * u[2] if u[0] == "p" else MH * DEC

        def sp_off(u):
            if u[0] == "p":
                return (u[1] % 2) * SPW + sum(SEQ - P * k for k in range(u[2] + 1, QB))
            return (CB - u[2]) * SH * DEC

        def head_end(s):
            u = s - 1 - LAG_PV
            if 0 <= u < NPU and u % QB == QB - 1:
                return u // QB
            return SH if u == NU - 1 else None

        names = ("w_hi w_lo p_done act_read dve_read vec_in trig_in act_step dve_step "
                 "sq_done acc_done rstd_done norm_done xn_hi xn_lo x_new zeroed "
                 "v_chunk v_raw v_hi v_lo v_st0 v_st1 k_raw k_st "
                 "z_done t_abs t_exp t_ln sp_raw sp_hi sp_lo cum_done a_raw a_hi a_lo pv_done o_hi o_lo "
                 "kc_in0 kc_in1 vc_in0 vc_in1 kc_hi kc_lo vc_hi vc_lo "
                 "c_raw c_ready c_hi c_lo c_st rope_done rope_hi rope_lo kr_st "
                 "s_done m_neg e_done p_scaled tr_done pt_hi pt_lo ol_mm ol_hi ol_lo "
                 "cs_in cs_hi cs_lo cc_in cc_hi cc_lo "
                 "ss_done ss_neg se_done ps_scaled str_done spt_hi spt_lo ols_mm ols_hi ols_lo "
                 "mi_raw mi_hi mi_lo f_raw conv0 conv2 gelu_done g_raw g_hi g_lo "
                 "p_in p_hi p_lo conv_st").split()

        with nc.Fori(0, DEPTH) as layer, ExitStack() as st:
            S = {n: st.enter_context(nc.semaphore(n)) for n in names}
            raw_in = [st.enter_context(nc.semaphore(f"raw_in{i}")) for i in range(RAW_SLOTS)]
            block = st.enter_context(nc.Block())

            @block.sync
            def _(sp_):
                state = [0]

                def load_to(n):
                    while state[0] < n:
                        c = state[0]
                        w = chunk_floats(CHUNKS[c])
                        if c >= RAW_SLOTS:
                            sp_.wait_ge(S["w_lo"], c - RAW_SLOTS + 1)
                        sp_.dma_start(raw[:, c % RAW_SLOTS, 0:w],
                                      wstream[layer, c, :, 0:w]).then_inc(raw_in[c % RAW_SLOTS], 16)
                        state[0] += 1

                load_to(1)
                sp_.dma_start(vv[:], vec[layer]).then_inc(S["vec_in"], 16)
                load_to(RAW_SLOTS)
                sp_.dma_start(mix[:, 0:2, 0:T], trig.rearrange("p (a t) -> p a t", a=2)).then_inc(S["trig_in"], 16)
                load_to(CHUNK_AT[("c", 0)] + 2)

                def load_k(i):
                    if i == 0:
                        sp_.wait_ge(S["v_st0"], 16 * ((QB + 2) // 2))
                        sp_.wait_ge(S["v_st1"], 16 * ((QB + 1) // 2))
                    if i >= 2:
                        sp_.wait_ge(S["kc_lo"], i - 1)
                    sp_.dma_start(kcraw[i % 2], kc[layer, CB - 1 - i]).then_inc(S[f"kc_in{i % 2}"], 16)

                def load_v(i):
                    if i == 0:
                        sp_.wait_ge(S["k_st"], 16 * PAIRS)
                    if i >= 2:
                        sp_.wait_ge(S["vc_lo"], i - 1)
                    sp_.dma_start(vcraw[i % 2], vc[layer, CB - 1 - i]).then_inc(S[f"vc_in{i % 2}"], 16)

                for i in range(2):
                    load_k(i)
                for i in range(2):
                    load_v(i)
                for i in range(2, 5):
                    load_k(i)
                for i in range(2, CB):
                    load_v(i)
                    if i + 3 < CB:
                        load_k(i + 3)
                load_to(CHUNK_AT[("ga", 0)] + RAW_SLOTS - 1)

                sp_.wait_ge(S["c_st"], 16)
                sp_.wait_ge(S["kr_st"], 16)
                sp_.wait_ge(S["tr_done"], NM)
                sp_.dma_start(craws[:, 0], cct[layer]).then_inc(S["cs_in"], 16)
                sp_.dma_start(craws[:, 1], krc[layer]).then_inc(S["cs_in"], 16)
                sp_.wait_ge(S["cs_lo"], 1)
                sp_.dma_start(craws[:, 0], cc[layer]).then_inc(S["cc_in"], 16)
                load_to(CHUNK_AT[("down", len(FFN_PARTS) - 1, 2)])
                sp_.wait_ge(S["conv2"], 2 * FT)
                sp_.dma_start(mix[:, 0:2, 0:T], p_in[layer].rearrange("(k p) t -> p k t", p=P)).then_inc(S["p_in"], 16)
                sp_.wait_ge(S["act_read"], aread(("upv", FT - 1)))
                sp_.dma_start(conv_out[layer], ctail[:]).then_inc(S["conv_st"], 16)
                load_to(len(CHUNKS))
                sp_.wait_ge(S["conv_st"], 16)

            @block.gpsimd
            def _(pool):
                for c, ch in enumerate(CHUNKS):
                    w = chunk_floats(ch)
                    dst = ukuv if ch[0] == "ukuv" else wsp[:, RING_AT[ch] % W_SLOTS]
                    pool.wait_ge(S["w_hi"], c + 1)
                    nc.gpsimd.tensor_tensor(dst[:, 1, 0:w], raw[:, c % RAW_SLOTS, 0:w], dst[:, 0, 0:w].bitcast(F32),
                                            ALU.subtract).then_inc(S["w_lo"], 1)

            @block.scalar
            def _(act):
                ac = nc.scalar.activation
                split = [0]

                def split_to(n):
                    while split[0] <= min(n, len(CHUNKS) - 1):
                        c = split[0]
                        ch = CHUNKS[c]
                        w = chunk_floats(ch)
                        act.wait_ge(raw_in[c % RAW_SLOTS], 16 * (c // RAW_SLOTS + 1))
                        dst = ukuv if ch[0] == "ukuv" else wsp[:, RING_AT[ch] % W_SLOTS]
                        if ch[0] != "ukuv" and RING_AT[ch] >= W_SLOTS:
                            old = RING[RING_AT[ch] - W_SLOTS]
                            if old[0] == "v":
                                act.wait_ge(S["v_chunk"], old[1] + 1)
                            else:
                                act.wait_ge(S["p_done"], AT[last_tile(old)] + 1)
                        ac(dst[:, 0, 0:w], raw[:, c % RAW_SLOTS, 0:w], ACT.Copy).then_inc(S["w_hi"], 1)
                        split[0] += 1

                def tile(t, chunk=None):
                    if chunk is not None:
                        split_to(CHUNK_AT[chunk] + 1)
                    act.wait_ge(S["p_done"], AT[t] + 1)
                    return ptile(AT[t])

                def bank(t):
                    act.wait_ge(S["p_done"], AT[t] + 1)
                    return ps[:, 2 * (AT[t] % 2)]

                def rsqrt(t, n):
                    z = tile(t)
                    ac(halves(rstd[:]), z, ACT.Ln, bias=epsb[:], scale=1.0 / n).then_inc(S["act_read"], 1)
                    act.wait_ge(S["act_read"], aread(t))
                    ac(rstd[:], rstd[:], ACT.Exp, scale=-0.5).then_inc(S["rstd_done"], 1)

                def square(n, src, sem="sq_done"):
                    if n >= 2:
                        act.wait_ge(S["acc_done"], n - 1)
                    ac(sq[n % 2] if src.ndim == 2 else halves(sq[n % 2]), src, ACT.Square).then_inc(S[sem], 1)

                def xn_hi(n0, j, src):
                    act.wait_ge(S["norm_done"], n0 + j + 1)
                    ac(xn[:, 0, j], src, ACT.Copy).then_inc(S["xn_hi"], 1)

                nc.scalar.preload_act_table_set("natural_log_exp_and_others")
                split_to(0)
                for j in range(KT):
                    square(j, xT[:, j])
                rsqrt(("nm", 0), D)
                split_to(1)
                for j in range(KT):
                    xn_hi(0, j, tmp[j % 2])

                split_to(5)
                act.wait_ge(S["v_chunk"], 4)
                for i in range(QB + 1):
                    if i >= 2:
                        act.wait_ge(S[f"v_st{i % 2}"], 16 * (i // 2))
                    ac(vraw[:, i % 2], ps[:, 3 + i], ACT.Copy).then_inc(S["v_raw"], 1)
                    ac(v_s[:, 0, i], ps[:, 3 + i], ACT.Copy).then_inc(S["v_hi"], 1)
                    act.wait_ge(S["v_raw"], i + 1)
                    if i < QB:
                        act.dma_start(v_out[layer, i * P:(i + 1) * P], vraw[:, i % 2]).then_inc(S[f"v_st{i % 2}"], 16)
                    else:
                        act.dma_start(v_out[layer, SEQ:T], vraw[P - DEC:P, i % 2]).then_inc(S[f"v_st{i % 2}"], 16)

                def qk_tile(t):
                    z = tile(t, t)
                    n = t[1]
                    if t[0] == "q":
                        for r in range(2):
                            ac(q_smp[64 * r:64 * r + 64, 0, n, DEC * r:DEC * r + DEC],
                               z[64 * r:64 * r + 64, 1, HT - DEC:HT], ACT.Copy, scale=SB_SCALE)
                        ac(halves(qk[:, n % 2, 0, 0]), z, ACT.Copy, scale=SB_SCALE).then_inc(S["act_read"], 1)
                    else:
                        if n > 0:
                            act.wait_ge(S["k_st"], 16 * n)
                        ac(halves(kraw), z, ACT.Copy).then_inc(S["k_raw"], 1)
                        ac(k_tail[:, 0, n], z[:, 1, HT - P:HT], ACT.Copy)
                        ac(halves(qk[:, n % 2, 1, 0]), z, ACT.Copy).then_inc(S["act_read"], 1)
                        act.wait_ge(S["k_raw"], n + 1)
                        act.dma_start(k_out[layer, n * P:(n + 1) * P], kraw).then_inc(S["k_st"], 16)

                act.wait_ge(S["zeroed"], 1)
                qk_tile(("q", 0))
                qk_tile(("k", 0))

                for s in range(NSTEP):
                    h = head_end(s)
                    if h is not None:
                        act.wait_ge(S["pv_done"], s - LAG_PV)
                        if h < SH:
                            r = 64 * (h % 2)
                            ac(o_sb[r:r + 64, 0, h // 2, 0:SEQ], ps[r:r + 64, OB], ACT.Copy).then_inc(S["o_hi"], 1)
                        else:
                            for r in range(2):
                                ins = ac(o_sb[64 * r:64 * r + 64, 0, :, SEQ:T],
                                         ps[64 * r:64 * r + 64, OB, 0:MH * DEC]
                                         .rearrange("p (t c) -> p t c", t=PAIRS)[:, :, DEC * r:DEC * r + DEC], ACT.Copy)
                            ins.then_inc(S["o_hi"], 1)
                    i = s + 1 - FIRST_CACHE
                    if 0 <= i < CB:
                        act.wait_ge(S[f"kc_in{i % 2}"], 16 * (i // 2 + 1))
                        act.wait_ge(S["z_done"], max(NPU, FIRST_CACHE + i - 3))
                        ac(kcs[:, 0, i % 4], kcraw[i % 2], ACT.Copy).then_inc(S["kc_hi"], 1)
                    i = s + 1 - FIRST_CACHE - LAG_PV
                    if 0 <= i < CB:
                        act.wait_ge(S[f"vc_in{i % 2}"], 16 * (i // 2 + 1))
                        act.wait_ge(S["pv_done"], max(NPU, FIRST_CACHE + i - 3))
                        ac(v_s[:, 0, i % 4], vcraw[i % 2], ACT.Copy).then_inc(S["vc_hi"], 1)
                    if s < NU:
                        w = width(units[s])
                        act.wait_ge(S["z_done"], s + 1)
                        if s >= 2:
                            act.wait_ge(S["sp_lo"], s - 1)
                        ac(tsp[:, s % 2, 0:w], ps[:, ZB + s % 3, 0:w], ACT.Abs).then_inc(S["t_abs"], 1)
                        act.wait_ge(S["t_abs"], s + 1)
                        ac(tsp[:, s % 2, 0:w], tsp[:, s % 2, 0:w], ACT.Exp, scale=-1.0).then_inc(S["t_exp"], 1)
                    if 1 <= s <= NU:
                        u, n = units[s - 1], s - 1
                        w1, o = width(u), sp_off(u)
                        act.wait_ge(S["sp_raw"], s)
                        if n >= 4:
                            act.wait_ge(S["cum_done"], n - 3)
                        ac(sp[:, 0, o:o + w1], tsp[:, n % 2, 0:w1], ACT.Copy).then_inc(S["sp_hi"], 1)
                    n = s - LAG_CUM
                    if 0 <= n < NU:
                        w2 = width(units[n])
                        act.wait_ge(S["cum_done"], n + 1)
                        if n >= 2:
                            act.wait_ge(S["a_lo"], n - 1)
                        ac(araw[:, n % 2, 0:w2], ps[:, ZB + n % 3, 0:w2], ACT.Exp).then_inc(S["a_raw"], 1)
                    if s < NU:
                        act.wait_ge(S["t_exp"], s + 1)
                        ac(tsp[:, s % 2, 0:w], tsp[:, s % 2, 0:w], ACT.Ln, bias=1.0).then_inc(S["t_ln"], 1)
                    if s in fill:
                        qk_tile(fill[s])

                z = tile(("c", 0), ("c", 0))
                ac(halves(craw), z, ACT.Copy).then_inc(S["c_raw"], 1)
                ac(halves(sq[0]), z, ACT.Square).then_inc(S["act_read"], 1)

                def rope_raw(n, t):
                    z = tile(t, t)
                    if n > 0:
                        act.wait_ge(S["rope_lo"], n)
                    if n == 1:
                        act.wait_ge(S["kr_st"], 16)
                    ac(halves(rope[0]), z, ACT.Copy).then_inc(S["act_read"], 1)

                def rope_parts(n):
                    act.wait_ge(S["rope_done"], n + 1)
                    if n == 0:
                        act.dma_start(kr_out[layer], rope[0][0:ROPE]).then_inc(S["kr_st"], 16)
                        ac(krT[:, 0], rope[0], ACT.Copy).then_inc(S["rope_hi"], 1)
                    else:
                        for a in range(4):
                            ac(qr_smp[32 * a:32 * a + 32, 0, n - 1, DEC * a:DEC * a + DEC],
                               rope[0][32 * a:32 * a + 32, SEQ:T], ACT.Copy)
                        ac(qr[:, 0, n - 1], rope[0], ACT.Copy).then_inc(S["rope_hi"], 1)

                rope_raw(0, ("kr", 0))
                rope_parts(0)
                rope_raw(1, ("qr", 0))
                act.wait_ge(S["zeroed"], 2)
                rope_parts(1)
                rope_raw(2, ("qr", 1))
                rope_parts(2)
                split_to(CHUNK_AT[("qn", 0)])
                rsqrt(("cn", 0), LORA)
                act.wait_ge(S["c_ready"], 1)
                act.dma_start(c_out[layer], craw).then_inc(S["c_st"], 16)
                ac(cT[:, 0], craw, ACT.Copy).then_inc(S["c_hi"], 1)
                n = AT[("ct", 0)]
                act.wait_ge(S["p_done"], n + 1)
                ac(ctok[:, 0, 0:QB], ps[:, 2 * (n % 2)].rearrange("p (b l) -> p b l", l=P), ACT.Copy)
                ac(ctok[:, 0, QB], ps[:, 2 * (n % 2) + 1, 0:P], ACT.Copy).then_inc(S["act_read"], 1)

                def m_tile(t):
                    if t[0] == "qn":
                        z = tile(t, t)
                        if t[1] > 0:
                            act.wait_ge(S["p_done"], AT[("ql", 2 * t[1] - 1)] + 1)
                        ac(halves(qn[:, 0]), z, ACT.Copy).then_inc(S["act_read"], 1)
                    elif t[0] == "ql":
                        z, h = bank(t), t[1]
                        if h > 0:
                            act.wait_ge(S["s_done"], QB * h)
                        ac(ql_smp[:, 0, h], ps[:, 2 * (AT[t] % 2) + 1, 0:DEC], ACT.Copy)
                        ac(ql[:, 0], z, ACT.Copy).then_inc(S["act_read"], 1)
                    else:
                        z, r = bank(t), 64 * (t[1] % 2)
                        ac(o_ml[r:r + 64, 0, t[1] // 2, 0:SEQ], z[r:r + 64], ACT.Copy).then_inc(S["act_read"], 1)

                for s in range(M_STEPS):
                    for t in m_tiles(s):
                        if t[0] != "uv":
                            m_tile(t)
                    n = s - 2
                    if 0 <= n < NM:
                        h, qb = m_units[n]
                        act.wait_ge(S["tr_done"], n + 1)
                        if h > 0:
                            act.wait_ge(S["ol_mm"], h)
                        ac(pt_view(0, qb), ps[:, ZB + 2, 0:P * (qb + 1)].rearrange("p (b q) -> p b q", q=P),
                           ACT.Copy).then_inc(S["pt_hi"], 1)
                    n = s - 1
                    if 0 <= n < NM:
                        w = P * (m_units[n][1] + 1)
                        act.wait_ge(S["m_neg"], n + 1)
                        if n >= 2:
                            act.wait_ge(S["tr_done"], n - 1)
                        ac(prw[:, n % 2, 0:w], ps[:, ZB + n % 2, 0:w], ACT.Exp, bias=negmax[:, n % 2:n % 2 + 1],
                           scale=MLA_SCALE, accum_out=rsum[:, n % 2:n % 2 + 1]).then_inc(S["e_done"], 1)
                    if s >= 3 and (s - 3) % QB == QB - 1 and s - 3 < NM:
                        h = (s - 3) // QB
                        act.wait_ge(S["ol_mm"], h + 1)
                        if h > 0:
                            act.wait_ge(S["p_done"], AT[("uv", h - 1)] + 1)
                        ac(ol[:, 0], ps[:, OB], ACT.Copy).then_inc(S["ol_hi"], 1)
                    for t in m_tiles(s):
                        if t[0] == "uv":
                            m_tile(t)

                act.wait_ge(S["cs_in"], 32)
                act.wait_ge(S["p_done"], AT[("uv", MH - 1)] + 1)
                ac(cache_s[:, 0], craws, ACT.Copy).then_inc(S["cs_hi"], 1)
                for g in range(2):
                    act.wait_ge(S["ss_neg"], g + 1)
                    if g > 0:
                        act.wait_ge(S["str_done"], g)
                    ac(psm, s_view, ACT.Exp, bias=negmax[:, g:g + 1], scale=MLA_SCALE,
                       accum_out=rsum[:, g:g + 1]).then_inc(S["se_done"], 1)
                    if g == 1:
                        act.wait_ge(S["cc_in"], 16)
                        act.wait_ge(S["ss_done"], 2)
                        ac(cache_s[:, 0, 0], craws[:, 0], ACT.Copy).then_inc(S["cc_hi"], 1)
                    act.wait_ge(S["str_done"], g + 1)
                    ac(pT_s[:, 0, :, g * P:(g + 1) * P], s_view.rearrange("p (b q) -> p b q", q=P),
                       ACT.Copy).then_inc(S["spt_hi"], 1)
                act.wait_ge(S["ols_mm"], 1)
                ac(ol_s[:, 0], ps[:, OB, 0:2 * P], ACT.Copy).then_inc(S["ols_hi"], 1)
                z = bank(("uvs", 0))
                for r in range(2):
                    ins = ac(o_ml[64 * r:64 * r + 64, 0, :, SEQ:T],
                             z[64 * r:64 * r + 64, 0:MH * DEC]
                             .rearrange("p (t c) -> p t c", t=PAIRS)[:, :, DEC * r:DEC * r + DEC], ACT.Copy)
                ins.then_inc(S["act_read"], 1)

                for j in range(KT):
                    for n, t in enumerate((("ga", j), ("gb", j))):
                        z = tile(t, t)
                        if j >= 2:
                            act.wait_ge(S["dve_read"], dread(("yb", j - 2)))
                        ac(halves(mix[:, 2 * n + j % 2, 0:T]), z, ACT.Sigmoid).then_inc(S["act_read"], 1)
                    split_to(CHUNK_AT[("proj", j)] + 1)
                    act.wait_ge(S["mi_raw"], j + 1)
                    ac(mixin[:, 0, j], tmp[0], ACT.Copy).then_inc(S["mi_hi"], 1)

                for j in range(KT):
                    z = tile(("out", j), ("out", j))
                    ac(halves(fT[:, j]), z, ACT.Copy).then_inc(S["f_raw"], 1)
                    if j == 0:
                        act.wait_ge(S["dve_read"], dread(("yb", KT - 1)))
                    square(KT + j, z, "act_read")
                nc.scalar.preload_act_table_set("natural_log_exp_and_others")
                rsqrt(("nm", 1), D)
                for j in range(KT):
                    act.wait_ge(S["x_new"], j + 1)
                    square(2 * KT + j, xT[:, j])
                rsqrt(("nm", 2), D)
                for j in range(KT):
                    xn_hi(KT, j, tmp[j % 2])

                def u_tile(t):
                    v, j = t[0] == "upv", t[1]
                    f, n = j + FT * v, 2 * j + v
                    z = tile(t, t)
                    e = uext[v]
                    if j > 0:
                        act.wait_ge(S["conv2"], n - 1)
                    ac(e[:, 2:2 + HT], z[:, 0], ACT.Copy)
                    ac(e[:, 2 + HT:2 + SEQ], z[:, 1, 0:SEQ - HT], ACT.Copy)
                    ac(e[:, 4 + SEQ:4 + T], z[:, 1, SEQ - HT:HT], ACT.Copy)
                    ac(e[:, 2 + SEQ:4 + SEQ], vv[:, V_ST + 2 * f:V_ST + 2 * f + 2], ACT.Copy)
                    b0 = 2 * (AT[t] % 2) + 1
                    ac(ctail[:, f].rearrange("p (a b) -> p a b", a=2),
                       ps[:, b0, SEQ - HT - 2:SEQ - HT - 2 + 2 * DEC].rearrange("p (a b) -> p a b", a=2)[:, :, 0:2],
                       ACT.Copy).then_inc(S["act_read"], 1)
                    act.wait_ge(S["act_read"], aread(t))
                    if v and j > 0:
                        act.wait_ge(S["g_raw"], j)
                    ac(uc[v], e[:, 0:T + 2], ACT.Identity, scale=vv[:, V_CW + f:V_CW + f + 1],
                       bias=vv[:, V_CB + f:V_CB + f + 1]).then_inc(S["conv0"], 1)

                def g_place(j):
                    i = 0 if j < _F0[1] else 1 if j < _F0[2] else 2
                    return i, g_s[i % 2], j - _F0[i]

                def g_high(j):
                    act.wait_ge(S["g_raw"], j + 1)
                    i, g, k = g_place(j)
                    if i == 2:
                        act.wait_ge(S["p_done"], AT[("down", 0, KT - 1)] + 1)
                    ac(g[:, 0, k], gt, ACT.Copy).then_inc(S["g_hi"], 1)

                act.wait_ge(S["zeroed"], 3)
                for part in (0, 1, "d0", 2, "d1", "d2"):
                    if part in (0, 1, 2):
                        for j in range(_F0[part], _F0[part + 1]):
                            u_tile(("upg", j))
                            if j > _F0[part]:
                                g_high(j - 1)
                            u_tile(("upv", j))
                            act.wait_ge(S["conv2"], 2 * j + 1)
                            ac(gel, uc[0], ACT.Gelu_apprx_tanh).then_inc(S["gelu_done"], 1)
                        g_high(_F0[part + 1] - 1)
                    elif part == "d0":
                        for j in range(KT):
                            z = tile(("down", 0, j), ("down", 0, j))
                            ac(halves(fT[:, j]), z, ACT.Copy).then_inc(S["act_read"], 1)
                    elif part == "d1":
                        for j in range(KT):
                            split_to(CHUNK_AT[("down", 1, j)] + 1)
                    else:
                        for j in range(KT):
                            split_to(CHUNK_AT[("down", 2, j)] + 1)
                            act.wait_ge(S["dve_read"], dread(("down", 2, j)))
                            square(3 * KT + j, fT[:, j])
                nc.scalar.preload_act_table_set("natural_log_exp_and_others")
                act.wait_ge(S["p_in"], 16)
                for k in range(PLE // P):
                    ac(p_s[:, 0, k], mix[:, k, 0:T], ACT.Copy).then_inc(S["p_hi"], 1)
                rsqrt(("nm", 3), D)
                for j in range(KT):
                    act.wait_ge(S["x_new"], KT + j + 1)
                    ac(xn[:, 0, j], xT[:, j], ACT.Copy).then_inc(S["xn_hi"], 1)

                for j in range(KT):
                    z = tile(("pleg", j), ("pleg", j))
                    if j >= 2:
                        act.wait_ge(S["dve_read"], dread(("plep", j - 2)))
                    ac(halves(mix[:, 2 + j % 2, 0:T]), z, ACT.Sigmoid).then_inc(S["act_read"], 1)
                    split_to(CHUNK_AT[("plep", j)] + 1)
                act.wait_ge(S["v_st0"], 16 * ((QB + 2) // 2))
                act.wait_ge(S["v_st1"], 16 * ((QB + 1) // 2))
                act.wait_ge(S["k_st"], 16 * PAIRS)
                act.wait_ge(S["c_st"], 16)
                act.wait_ge(S["kr_st"], 16)

            @block.vector
            def _(dve):
                v = nc.vector
                steps = [0]

                def link(ins):
                    steps[0] += 1
                    ins.then_inc(S["dve_step"], 1)
                    dve.wait_ge(S["dve_step"], steps[0])

                def lo(dst, src, hi, sem, scale=1.0):
                    ins = v.scalar_tensor_tensor(dst, src, scale, hi.bitcast(F32), ALU.mult, ALU.subtract)
                    if sem is not None:
                        ins.then_inc(S[sem], 1)

                def add_squares(n, sem, count):
                    dve.wait_ge(S[sem], count)
                    if n % KT == 0:
                        v.tensor_copy(acc[:], sq[n % 2]).then_inc(S["acc_done"], 1)
                    else:
                        dve.wait_ge(S["acc_done"], n)
                        v.tensor_tensor(acc[:], acc[:], sq[n % 2], ALU.add).then_inc(S["acc_done"], 1)

                def normed(n0, gain, which):
                    dve.wait_ge(S["rstd_done"], which)
                    for j in range(KT + 1):
                        if j < KT:
                            if j >= 2:
                                dve.wait_ge(S["xn_lo"], n0 + j - 1)
                            v.scalar_tensor_tensor(tmp[j % 2], xT[:, j], vv[:, gain + j:gain + j + 1], rstd[:],
                                                   ALU.mult, ALU.mult).then_inc(S["norm_done"], 1)
                        if j > 0:
                            dve.wait_ge(S["xn_hi"], n0 + j)
                            lo(xn[:, 1, j - 1], tmp[(j - 1) % 2], xn[:, 0, j - 1], "xn_lo")

                v.memset(q_smp.bitcast(F32), 0.0).then_inc(S["zeroed"], 1)
                for j in range(KT):
                    add_squares(j, "sq_done", j + 1)
                dve.wait_ge(S["vec_in"], 16)
                normed(0, V_GPM, 1)

                for i in range(QB + 1):
                    dve.wait_ge(S["v_hi"], i + 1)
                    lo(v_s[:, 1, i], ps[:, 3 + i], v_s[:, 0, i], "v_lo")

                def qk_tile(t):
                    n = t[1]
                    dve.wait_ge(S["act_read"], aread(t))
                    z = ptile(AT[t])
                    if t[0] == "q":
                        for r in range(2):
                            lo(q_smp[64 * r:64 * r + 64, 1, n, DEC * r:DEC * r + DEC],
                               z[64 * r:64 * r + 64, 1, HT - DEC:HT],
                               q_smp[64 * r:64 * r + 64, 0, n, DEC * r:DEC * r + DEC], None, SB_SCALE)
                        lo(halves(qk[:, n % 2, 0, 1]), z, halves(qk[:, n % 2, 0, 0]), "dve_read", SB_SCALE)
                    else:
                        lo(k_tail[:, 1, n], z[:, 1, HT - P:HT], k_tail[:, 0, n], None)
                        lo(halves(qk[:, n % 2, 1, 1]), z, halves(qk[:, n % 2, 1, 0]), "dve_read")

                qk_tile(("q", 0))
                qk_tile(("k", 0))

                for s in range(NSTEP):
                    h = head_end(s)
                    if h is not None:
                        dve.wait_ge(S["o_hi"], h + 1)
                        if h < SH:
                            r = 64 * (h % 2)
                            lo(o_sb[r:r + 64, 1, h // 2, 0:SEQ], ps[r:r + 64, OB], o_sb[r:r + 64, 0, h // 2, 0:SEQ], "o_lo")
                        else:
                            for r in range(2):
                                lo(o_sb[64 * r:64 * r + 64, 1, :, SEQ:T],
                                   ps[64 * r:64 * r + 64, OB, 0:MH * DEC]
                                   .rearrange("p (t c) -> p t c", t=PAIRS)[:, :, DEC * r:DEC * r + DEC],
                                   o_sb[64 * r:64 * r + 64, 0, :, SEQ:T], "o_lo" if r else None)
                    i = s + 1 - FIRST_CACHE
                    if 0 <= i < CB:
                        dve.wait_ge(S["kc_hi"], i + 1)
                        lo(kcs[:, 1, i % 4], kcraw[i % 2], kcs[:, 0, i % 4], "kc_lo")
                    i = s + 1 - FIRST_CACHE - LAG_PV
                    if 0 <= i < CB:
                        dve.wait_ge(S["vc_hi"], i + 1)
                        lo(v_s[:, 1, i % 4], vcraw[i % 2], v_s[:, 0, i % 4], "vc_lo")
                    w = width(units[s]) if s < NU else 0
                    if 1 <= s <= NU:
                        u, n = units[s - 1], s - 1
                        w1, o = width(u), sp_off(u)
                        dve.wait_ge(S["sp_hi"], s)
                        lo(sp[:, 1, o:o + w1], tsp[:, n % 2, 0:w1], sp[:, 0, o:o + w1], "sp_lo")
                    n = s - LAG_CUM
                    if 0 <= n < NU:
                        w2 = width(units[n])
                        dve.wait_ge(S["a_raw"], n + 1)
                        if n >= 2:
                            dve.wait_ge(S["pv_done"], n - 1)
                        v.tensor_copy(att[:, n % 2, 0, 0:w2], araw[:, n % 2, 0:w2]).then_inc(S["a_hi"], 1)
                        dve.wait_ge(S["a_hi"], n + 1)
                        lo(att[:, n % 2, 1, 0:w2], araw[:, n % 2, 0:w2], att[:, n % 2, 0, 0:w2], "a_lo")
                    if s < NU:
                        dve.wait_ge(S["t_ln"], s + 1)
                        v.scalar_tensor_tensor(tsp[:, s % 2, 0:w], ps[:, ZB + s % 3, 0:w], 0.0, tsp[:, s % 2, 0:w],
                                               ALU.max, ALU.add).then_inc(S["sp_raw"], 1)
                    if s in fill:
                        qk_tile(fill[s])

                def rope_parts(n, t):
                    dve.wait_ge(S["act_read"], aread(t))
                    if n == 0:
                        dve.wait_ge(S["trig_in"], 16)
                    link(v.stream_shuffle(rope[1], rope[0], _q_swap()))
                    link(v.tensor_tensor(rope[1], rope[1], sin, ALU.mult))
                    link(v.tensor_tensor(rope[0], rope[0], cos, ALU.mult))
                    v.tensor_tensor(rope[0], rope[0], rope[1], ALU.add).then_inc(S["rope_done"], 1)
                    dve.wait_ge(S["rope_hi"], n + 1)
                    if n == 0:
                        lo(krT[:, 1], rope[0], krT[:, 0], "rope_lo")
                    else:
                        for a in range(4):
                            lo(qr_smp[32 * a:32 * a + 32, 1, n - 1, DEC * a:DEC * a + DEC],
                               rope[0][32 * a:32 * a + 32, SEQ:T],
                               qr_smp[32 * a:32 * a + 32, 0, n - 1, DEC * a:DEC * a + DEC], None)
                        lo(qr[:, 1, n - 1], rope[0], qr[:, 0, n - 1], "rope_lo")

                rope_parts(0, ("kr", 0))
                v.memset(qr_smp.bitcast(F32), 0.0).then_inc(S["zeroed"], 1)
                dve.wait_ge(S["zeroed"], 2)
                rope_parts(1, ("qr", 0))
                rope_parts(2, ("qr", 1))
                dve.wait_ge(S["rstd_done"], 2)
                v.scalar_tensor_tensor(craw, craw, vv[:, V_CG:V_CG + 1], rstd[:], ALU.mult, ALU.mult).then_inc(S["c_ready"], 1)
                dve.wait_ge(S["c_hi"], 1)
                lo(cT[:, 1], craw, cT[:, 0], "c_lo")
                dve.wait_ge(S["act_read"], aread(("ct", 0)))
                n = AT[("ct", 0)]
                lo(ctok[:, 1, 0:QB], ps[:, 2 * (n % 2)].rearrange("p (b l) -> p b l", l=P), ctok[:, 0, 0:QB], None)
                lo(ctok[:, 1, QB], ps[:, 2 * (n % 2) + 1, 0:P], ctok[:, 0, QB], "dve_read")

                def m_tile(t):
                    dve.wait_ge(S["act_read"], aread(t))
                    z = ps[:, 2 * (AT[t] % 2)]
                    if t[0] == "qn":
                        lo(halves(qn[:, 1]), ptile(AT[t]), halves(qn[:, 0]), "dve_read")
                    elif t[0] == "ql":
                        h = t[1]
                        lo(ql_smp[:, 1, h], ps[:, 2 * (AT[t] % 2) + 1, 0:DEC], ql_smp[:, 0, h], None)
                        lo(ql[:, 1], z, ql[:, 0], "dve_read")
                    else:
                        r = 64 * (t[1] % 2)
                        lo(o_ml[r:r + 64, 1, t[1] // 2, 0:SEQ], z[r:r + 64], o_ml[r:r + 64, 0, t[1] // 2, 0:SEQ], "dve_read")

                for s in range(M_STEPS):
                    for t in m_tiles(s):
                        if t[0] != "uv":
                            m_tile(t)
                    n = s - 1
                    if 0 <= n < NM:
                        i, w = n % 2, P * (m_units[n][1] + 1)
                        dve.wait_ge(S["s_done"], n + 1)
                        link(v.reduce_max(negmax[:, i:i + 1], ps[:, ZB + i, 0:w], mybir.AxisListType.X))
                        v.tensor_scalar(negmax[:, i:i + 1], negmax[:, i:i + 1], -MLA_SCALE, None,
                                        ALU.mult).then_inc(S["m_neg"], 1)
                    n2 = s - 2
                    if 0 <= n2 < NM:
                        qb = m_units[n2][1]
                        dve.wait_ge(S["pt_hi"], n2 + 1)
                        lo(pt_view(1, qb), ps[:, ZB + 2, 0:P * (qb + 1)].rearrange("p (b q) -> p b q", q=P),
                           pt_view(0, qb), "pt_lo")
                    if 0 <= n < NM:
                        dve.wait_ge(S["e_done"], n + 1)
                        link(v.reciprocal(rsum[:, i:i + 1], rsum[:, i:i + 1]))
                        v.tensor_scalar(prw[:, i, 0:w], prw[:, i, 0:w], rsum[:, i:i + 1], None,
                                        ALU.mult).then_inc(S["p_scaled"], 1)
                    if s >= 3 and (s - 3) % QB == QB - 1 and s - 3 < NM:
                        dve.wait_ge(S["ol_hi"], (s - 3) // QB + 1)
                        lo(ol[:, 1], ps[:, OB], ol[:, 0], "ol_lo")
                    for t in m_tiles(s):
                        if t[0] == "uv":
                            m_tile(t)

                dve.wait_ge(S["cs_hi"], 1)
                lo(cache_s[:, 1], craws, cache_s[:, 0], "cs_lo")
                for g in range(2):
                    dve.wait_ge(S["ss_done"], g + 1)
                    link(v.reduce_max(negmax[:, g:g + 1], s_view, mybir.AxisListType.X))
                    v.tensor_scalar(negmax[:, g:g + 1], negmax[:, g:g + 1], -MLA_SCALE, None,
                                    ALU.mult).then_inc(S["ss_neg"], 1)
                    dve.wait_ge(S["se_done"], g + 1)
                    link(v.reciprocal(rsum[:, g:g + 1], rsum[:, g:g + 1]))
                    v.tensor_scalar(psm, psm, rsum[:, g:g + 1], None, ALU.mult).then_inc(S["ps_scaled"], 1)
                    if g == 1:
                        dve.wait_ge(S["cc_hi"], 1)
                        lo(cache_s[:, 1, 0], craws[:, 0], cache_s[:, 0, 0], "cc_lo")
                    dve.wait_ge(S["spt_hi"], g + 1)
                    lo(pT_s[:, 1, :, g * P:(g + 1) * P], s_view.rearrange("p (b q) -> p b q", q=P),
                       pT_s[:, 0, :, g * P:(g + 1) * P], "spt_lo")
                dve.wait_ge(S["ols_hi"], 1)
                lo(ol_s[:, 1], ps[:, OB, 0:2 * P], ol_s[:, 0], "ols_lo")
                dve.wait_ge(S["act_read"], aread(("uvs", 0)))
                z = ps[:, 2 * (AT[("uvs", 0)] % 2)]
                for r in range(2):
                    lo(o_ml[64 * r:64 * r + 64, 1, :, SEQ:T],
                       z[64 * r:64 * r + 64, 0:MH * DEC]
                       .rearrange("p (t c) -> p t c", t=PAIRS)[:, :, DEC * r:DEC * r + DEC],
                       o_ml[64 * r:64 * r + 64, 0, :, SEQ:T], "dve_read" if r else None)

                for j in range(KT):
                    for n, (t, g) in enumerate(((("ya", j), ("ga", j)), (("yb", j), ("gb", j)))):
                        dve.wait_ge(S["act_read"], aread(g))
                        dve.wait_ge(S["p_done"], AT[t] + 1)
                        if n == 0 and j > 0:
                            dve.wait_ge(S["mi_lo"], j)
                        v.tensor_tensor(halves(tmp[n]), ptile(AT[t]), halves(mix[:, 2 * n + j % 2, 0:T]),
                                        ALU.mult).then_inc(S["dve_read"], 1)
                    dve.wait_ge(S["dve_read"], dread(("yb", j)))
                    v.tensor_tensor(tmp[0], tmp[0], tmp[1], ALU.add).then_inc(S["mi_raw"], 1)
                    dve.wait_ge(S["mi_hi"], j + 1)
                    lo(mixin[:, 1, j], tmp[0], mixin[:, 0, j], "mi_lo")
                for j in range(KT):
                    add_squares(KT + j, "act_read", aread(("out", j)))

                def residual(gain, which, n0, m0):
                    dve.wait_ge(S["rstd_done"], which)
                    for j in range(KT):
                        if j >= 2:
                            dve.wait_ge(S["x_new"], m0 + j - 1)
                        link(v.scalar_tensor_tensor(tmp[j % 2], fT[:, j], vv[:, gain + j:gain + j + 1], rstd[:],
                                                    ALU.mult, ALU.mult))
                        v.tensor_tensor(xT[:, j], xT[:, j], tmp[j % 2], ALU.add).then_inc(S["x_new"], 1)
                        if n0 is not None and j > 0:
                            add_squares(n0 + j - 1, "sq_done", n0 - KT + j)
                    if n0 is not None:
                        add_squares(n0 + KT - 1, "sq_done", n0)

                dve.wait_ge(S["f_raw"], KT)
                residual(V_GQM, 3, 2 * KT, 0)
                v.memset(mix[:, 0:2, 0:2], 0.0).then_inc(S["zeroed"], 1)
                normed(KT, V_GPF, 4)

                def taps(t):
                    w, j = t[0] == "upv", t[1]
                    f, n = j + FT * w, 2 * j + w
                    dve.wait_ge(S["conv0"], n + 1)
                    link(v.scalar_tensor_tensor(uc[w], uext[w][:, 1:T + 3], vv[:, V_CW + 2 * FT + f:V_CW + 2 * FT + f + 1],
                                                uc[w], ALU.mult, ALU.add))
                    v.scalar_tensor_tensor(uc[w], uext[w][:, 2:T + 4], vv[:, V_CW + 4 * FT + f:V_CW + 4 * FT + f + 1],
                                           uc[w], ALU.mult, ALU.add).then_inc(S["conv2"], 1)

                def g_low(part, j):
                    dve.wait_ge(S["g_hi"], j + 1)
                    lo(g_s[part % 2][:, 1, j - _F0[part]], gt, g_s[part % 2][:, 0, j - _F0[part]], "g_lo")

                for part in (0, 1, "d0", 2, "d1", "d2"):
                    if part in (0, 1, 2):
                        for j in range(_F0[part], _F0[part + 1]):
                            taps(("upg", j))
                            if j > _F0[part]:
                                g_low(part, j - 1)
                            taps(("upv", j))
                            dve.wait_ge(S["gelu_done"], j + 1)
                            dve.wait_ge(S["conv2"], 2 * j + 2)
                            v.tensor_tensor(gt[:, 0:SEQ], gel[:, 0:SEQ], uc[1][:, 0:SEQ], ALU.mult)
                            v.tensor_tensor(gt[:, SEQ:T], gel[:, SEQ + 2:T + 2], uc[1][:, SEQ + 2:T + 2],
                                            ALU.mult).then_inc(S["g_raw"], 1)
                        g_low(part, _F0[part + 1] - 1)
                    elif part != "d0":
                        i = int(part[1])
                        for j in range(KT):
                            t = ("down", i, j)
                            if i == 1:
                                dve.wait_ge(S["act_read"], aread(("down", 0, j)))
                            else:
                                dve.wait_ge(S["dve_read"], dread(("down", 1, j)))
                            dve.wait_ge(S["p_done"], AT[t] + 1)
                            v.tensor_tensor(halves(fT[:, j]), ptile(AT[t]), halves(fT[:, j]), ALU.add).then_inc(S["dve_read"], 1)
                            if i == 2 and j > 0:
                                add_squares(3 * KT + j - 1, "sq_done", 2 * KT + j)
                add_squares(4 * KT - 1, "sq_done", 3 * KT)
                for k in range(PLE // P):
                    dve.wait_ge(S["p_hi"], k + 1)
                    lo(p_s[:, 1, k], mix[:, k, 0:T], p_s[:, 0, k], "p_lo")
                residual(V_GQF, 5, None, KT)
                for j in range(KT):
                    dve.wait_ge(S["xn_hi"], 2 * KT + j + 1)
                    lo(xn[:, 1, j], xT[:, j], xn[:, 0, j], "xn_lo")

                for j in range(KT):
                    dve.wait_ge(S["act_read"], aread(("pleg", j)))
                    dve.wait_ge(S["p_done"], AT[("plep", j)] + 1)
                    if j >= 2:
                        dve.wait_ge(S["x_new"], 2 * KT + j - 1)
                    v.tensor_tensor(halves(tmp[j % 2]), ptile(AT[("plep", j)]), halves(mix[:, 2 + j % 2, 0:T]),
                                    ALU.mult).then_inc(S["dve_read"], 1)
                    dve.wait_ge(S["dve_read"], dread(("plep", j)))
                    v.tensor_tensor(xT[:, j], xT[:, j], tmp[j % 2], ALU.add).then_inc(S["x_new"], 1)
                dve.wait_ge(S["x_new"], 3 * KT)

            @block.tensor
            def _(pe):
                PARTS = ((0, 0), (0, 1), (1, 0))

                def banks_free(t):
                    n = AT[t]
                    if n >= 2:
                        if act_upto[n - 1]:
                            pe.wait_ge(S["act_read"], act_upto[n - 1])
                        if dve_upto[n - 1]:
                            pe.wait_ge(S["dve_read"], dve_upto[n - 1])

                def project(t, chunk, rhs, nk, k0=0, ready=None):
                    banks_free(t)
                    pe.wait_ge(S["w_lo"], CHUNK_AT[chunk] + 1)
                    w = wsp[:, RING_AT[chunk] % W_SLOTS]
                    z = ptile(AT[t])
                    for k in range(nk):
                        if ready is not None:
                            pe.wait_ge(S[ready[0]], ready[1] + k + 1)
                        for x, y in PARTS:
                            for h in range(2):
                                mm = pe.matmul(z[:, h], w[:, x, (k0 + k) * P:(k0 + k + 1) * P],
                                               rhs[:, y, k, h * HT:(h + 1) * HT],
                                               start=(k == 0 and (x, y) == (0, 0)), stop=(k == nk - 1 and x == 1))
                    mm.then_inc(S["p_done"], 1)

                def sums(t, src):
                    banks_free(t)
                    z = ptile(AT[t])
                    for h in range(2):
                        mm = pe.matmul(z[:, h], ones, src[:, h * HT:(h + 1) * HT], start=True, stop=True)
                    mm.then_inc(S["p_done"], 1)

                pe.wait_ge(S["acc_done"], KT)
                sums(("nm", 0), acc)
                for c in range(4):
                    pe.wait_ge(S["w_lo"], c + 1)
                    w = wsp[:, RING_AT[("v", c)] % W_SLOTS]
                    for k in range(2 * c, 2 * c + 2):
                        pe.wait_ge(S["xn_lo"], k + 1)
                        for i in range(QB + 1):
                            cols = slice(i * P, (i + 1) * P) if i < QB else slice(TAIL, T)
                            for x, y in PARTS:
                                mm = pe.matmul(ps[:, 3 + i], xn[:, x, k, cols], w[:, y, (k % 2) * 512:(k % 2 + 1) * 512],
                                               start=(k == 0 and (x, y) == (0, 0)), stop=(k == KT - 1 and x == 1))
                    mm.then_inc(S["v_chunk"], 1)
                pe.wait_ge(S["v_lo"], 1)
                project(("q", 0), ("q", 0), xn, KT)
                project(("k", 0), ("k", 0), xn, KT)
                pe.wait_ge(S["v_lo"], QB + 1)

                def sb_scores(n):
                    u = units[n]
                    z, w = ps[:, ZB + n % 3], width(u)
                    if n >= 3:
                        pe.wait_ge(S["a_raw"], n - 2)
                    if u[0] == "p":
                        _, h, kb = u
                        t, r = h // 2, 64 * (h % 2)
                        if h % 2 == 0 and kb == QB - 1:
                            pe.wait_ge(S["dve_read"], dread(("k", t)))
                        for i, (x, y) in enumerate(PARTS):
                            mm = pe.matmul(z[:, 0:w], qk[r:r + 64, t % 2, 1, x, kb * P:(kb + 1) * P],
                                           qk[r:r + 64, t % 2, 0, y, kb * P:SEQ], start=(i == 0), stop=False,
                                           skip_group_check=True)
                        mm = pe.matmul(z[:, 0:P], ident_b, masks[:, 1], start=False, stop=True, skip_group_check=True)
                    else:
                        kb = u[2]
                        if kb < CB:
                            pe.wait_ge(S["kc_lo"], CB - kb)
                        for t in range(PAIRS):
                            for i, (x, y) in enumerate(PARTS):
                                k = k_tail[:, x, t] if kb == CB else kcs[:, x, (CB - 1 - kb) % 4, t * P:(t + 1) * P]
                                mm = pe.matmul(z[:, 64 * t:64 * t + 64], k, q_smp[:, y, t],
                                               start=(t == 0 and i == 0), stop=(i == 2 and t == PAIRS - 1),
                                               skip_group_check=True)
                        if kb == CB:
                            mm = pe.matmul(z[:, 0:2 * P], ident_b, masks[:, 2:4], start=False, stop=True,
                                           skip_group_check=True)
                    mm.then_inc(S["z_done"], 1)

                def sb_sums(n):
                    u = units[n]
                    z, w = ps[:, ZB + n % 3], width(u)
                    pe.wait_ge(S["sp_lo"], n + 1)
                    first = n - (QB - 1 - u[2]) if u[0] == "p" else NPU
                    for x in range(2):
                        for m in range(first, n):
                            o, w2 = sp_off(units[m]), width(units[m])
                            pe.matmul(z[:, w - w2:w], exact[:, 1], sp[:, x, o:o + w2], start=False, stop=False,
                                      skip_group_check=True)
                        mm = pe.matmul(z[:, 0:w], exact[:, 0], sp[:, x, sp_off(u):sp_off(u) + w],
                                       start=False, stop=(x == 1), skip_group_check=True)
                    mm.then_inc(S["cum_done"], 1)

                def sb_pv(n):
                    u = units[n]
                    w = width(u)
                    pe.wait_ge(S["a_lo"], n + 1)
                    if u[0] == "p":
                        _, h, kb = u
                        if kb == QB - 1 and h > 0:
                            pe.wait_ge(S["o_lo"], h)
                        t = h // 2
                        for i, (x, y) in enumerate(PARTS):
                            mm = pe.matmul(ps[:, OB, SEQ - w:SEQ], v_s[:, x, kb, t * P:(t + 1) * P], att[:, n % 2, y, 0:w],
                                           start=(kb == QB - 1 and i == 0), stop=(kb == 0 and i == 2), skip_group_check=True)
                    else:
                        kb = u[2]
                        if kb == CB:
                            pe.wait_ge(S["o_lo"], SH)
                        else:
                            pe.wait_ge(S["vc_lo"], CB - kb)
                        for t in range(PAIRS):
                            for i, (x, y) in enumerate(PARTS):
                                slot = QB if kb == CB else (CB - 1 - kb) % 4
                                mm = pe.matmul(ps[:, OB, 64 * t:64 * t + 64], v_s[:, x, slot, t * P:(t + 1) * P],
                                               att[:, n % 2, y, 64 * t:64 * t + 64],
                                               start=(kb == CB and t == 0 and i == 0),
                                               stop=(kb == 0 and t == PAIRS - 1 and i == 2), skip_group_check=True)
                    mm.then_inc(S["pv_done"], 1)

                for s in range(NSTEP - 1):
                    if s < NU:
                        sb_scores(s)
                    if s in fill:
                        project(fill[s], fill[s], xn, KT)
                    if 0 <= s - LAG_CUM < NU:
                        sb_sums(s - LAG_CUM)
                    if 0 <= s - LAG_PV < NU:
                        sb_pv(s - LAG_PV)

                for t in (("c", 0), ("kr", 0), ("qr", 0), ("qr", 1)):
                    project(t, t, xn, KT)
                pe.wait_ge(S["act_read"], aread(("c", 0)))
                sums(("cn", 0), sq[0])
                pe.wait_ge(S["c_ready"], 1)
                banks_free(("ct", 0))
                n = AT[("ct", 0)]
                for i in range(QB + 1):
                    cols = slice(i * P, (i + 1) * P) if i < QB else slice(TAIL, T)
                    mm = pe.transpose(ps[:, 2 * (n % 2) + i // QB, (i % QB) * P:(i % QB + 1) * P], craw[:, cols], ident)
                mm.then_inc(S["p_done"], 1)

                def m_tile(t):
                    if t[0] == "qn":
                        project(t, t, xn, KT)
                        return
                    banks_free(t)
                    z, h = ps[:, 2 * (AT[t] % 2)], t[1]
                    r, p0 = 64 * (h % 2), h // 2 * P
                    if t[0] == "ql":
                        pe.wait_ge(S["w_lo"], CHUNK_AT[("ukuv", 0)] + 1)
                        pe.wait_ge(S["dve_read"], dread(("qn", h // 2)))
                        for i, (x, y) in enumerate(PARTS):
                            pe.matmul(z, ukuv[r:r + 64, x, p0:p0 + P], qn[r:r + 64, y, 0:SEQ], start=(i == 0), stop=(i == 2))
                        for i, (x, y) in enumerate(PARTS):
                            mm = pe.matmul(ps[:, 2 * (AT[t] % 2) + 1, 0:DEC], ukuv[r:r + 64, x, p0:p0 + P],
                                           qn[r:r + 64, y, SEQ:T], start=(i == 0), stop=(i == 2))
                    else:
                        pe.wait_ge(S["ol_lo"], h + 1)
                        for i, (x, y) in enumerate(PARTS):
                            mm = pe.matmul(z, ukuv[:, x, 512 + p0:512 + p0 + P], ol[:, y], start=(i == 0), stop=(i == 2))
                    mm.then_inc(S["p_done"], 1)

                for s in range(M_STEPS):
                    for t in m_tiles(s):
                        if t[0] != "uv":
                            m_tile(t)
                    n = s - 2
                    if 0 <= n < NM:
                        h, qb = m_units[n]
                        pe.wait_ge(S["p_scaled"], n + 1)
                        if n > 0:
                            pe.wait_ge(S["pt_lo"], n)
                        for kb in range(qb + 1):
                            mm = pe.transpose(ps[:, ZB + 2, kb * P:(kb + 1) * P], prw[:, n % 2, kb * P:(kb + 1) * P], ident)
                        mm.then_inc(S["tr_done"], 1)
                    if s >= 3 and (s - 3) % QB == QB - 1 and s - 3 < NM:
                        h = (s - 3) // QB
                        pe.wait_ge(S["pt_lo"], QB * (h + 1))
                        if h > 0:
                            pe.wait_ge(S["ol_lo"], h)
                        for kb in range(QB):
                            o = kb * PTS
                            for x, y in PARTS:
                                mm = pe.matmul(ps[:, OB, kb * P:SEQ], ctok[:, x, kb], pT[:, y, o + kb * P:o + SEQ],
                                               start=(kb == 0 and (x, y) == (0, 0)), stop=(kb == QB - 1 and x == 1))
                        mm.then_inc(S["ol_mm"], 1)
                    for t in m_tiles(s):
                        if t[0] == "uv":
                            m_tile(t)
                    if s < NM:
                        h, qb = m_units[s]
                        a, g, w = 32 * (h % 4), h // 4, P * (qb + 1)
                        z = ps[:, ZB + s % 2, 0:w]
                        pe.wait_ge(S["dve_read"], dread(("ql", h)))
                        if s == 0:
                            pe.wait_ge(S["rope_lo"], 3)
                            pe.wait_ge(S["c_lo"], 1)
                        if s >= 2:
                            pe.wait_ge(S["e_done"], s - 1)
                        for i, (x, y) in enumerate(PARTS):
                            pe.matmul(z, ql[:, x, qb * P:(qb + 1) * P], cT[:, y, 0:w], start=(i == 0), stop=False,
                                      skip_group_check=True)
                        for i, (x, y) in enumerate(PARTS):
                            pe.matmul(z, qr[a:a + 32, x, g, qb * P:(qb + 1) * P], krT[a:a + 32, y, 0:w], start=False, stop=False,
                                      tile_position=(a, 0), skip_group_check=True)
                        pe.matmul(z[:, qb * P:w], ident_b, masks[:, 4], start=False, stop=True,
                                  skip_group_check=True).then_inc(S["s_done"], 1)

                pe.wait_ge(S["cs_lo"], 1)
                for g in range(2):
                    if g > 0:
                        pe.wait_ge(S["spt_lo"], g)
                    for c in range(3):
                        z = ps[:, ZB + c] if c < 2 else ps[:, ZB + 2, 0:P]
                        ck = [(cache_s[:, y, 0, c * 512:(c + 1) * 512] if c < 2 else cT[:, y, TAIL:T]) for y in range(2)]
                        rk = [(cache_s[:, y, 1, c * 512:(c + 1) * 512] if c < 2 else krT[:, y, TAIL:T]) for y in range(2)]
                        for i, (x, y) in enumerate(PARTS):
                            pe.matmul(z, ql_smp[:, x, 4 * g:4 * g + 4], ck[y], start=(i == 0), stop=False)
                        for i, (x, y) in enumerate(PARTS):
                            mm = pe.matmul(z, qr_smp[:, x, g], rk[y], start=False, stop=(i == 2 and c < 2))
                        if c == 2:
                            mm = pe.matmul(z, ident_b, masks[:, 5], start=False, stop=True)
                    mm.then_inc(S["ss_done"], 1)
                    pe.wait_ge(S["ps_scaled"], g + 1)
                    for kb in range(CB + 1):
                        mm = pe.transpose(ps[:, ZB + kb // 4, (kb % 4) * P:(kb % 4 + 1) * P], psm[:, kb * P:(kb + 1) * P], ident)
                    mm.then_inc(S["str_done"], 1)
                pe.wait_ge(S["spt_lo"], 2)
                pe.wait_ge(S["cc_lo"], 1)
                for kb in range(CB + 1):
                    for x, y in PARTS:
                        c = cache_s[:, x, 0, kb * P:(kb + 1) * P] if kb < CB else ctok[:, x, QB]
                        mm = pe.matmul(ps[:, OB, 0:2 * P], c, pT_s[:, y, kb], start=(kb == 0 and (x, y) == (0, 0)),
                                       stop=(kb == CB and x == 1))
                mm.then_inc(S["ols_mm"], 1)
                banks_free(("uvs", 0))
                pe.wait_ge(S["ols_lo"], 1)
                for t in range(PAIRS):
                    for i, (x, y) in enumerate(PARTS):
                        mm = pe.matmul(ps[:, 2 * (AT[("uvs", 0)] % 2), 64 * t:64 * t + 64],
                                       ukuv[:, x, 512 + t * P:512 + (t + 1) * P], ol_s[:, y, 64 * t:64 * t + 64],
                                       start=(i == 0), stop=(i == 2))
                mm.then_inc(S["p_done"], 1)

                for j in range(KT):
                    project(("ga", j), ("ga", j), xn, KT)
                    project(("gb", j), ("gb", j), xn, KT)
                    project(("ya", j), ("proj", j), o_sb, PAIRS)
                    if j == 0:
                        pe.wait_ge(S["dve_read"], dread(("uvs", 0)))
                    project(("yb", j), ("proj", j), o_ml, PAIRS, PAIRS)
                for j in range(KT):
                    project(("out", j), ("out", j), mixin, KT, ready=("mi_lo", 0) if j == 0 else None)
                for n in (1, 2):
                    pe.wait_ge(S["acc_done"], KT * (n + 1))
                    sums(("nm", n), acc)

                for part in (0, 1, "d0", 2, "d1", "d2"):
                    if part in (0, 1, 2):
                        for t in _up(part):
                            project(t, t, xn, KT, ready=("xn_lo", KT) if t == ("upg", 0) else None)
                    else:
                        i = int(part[1])
                        for j in range(KT):
                            project(("down", i, j), ("down", i, j), g_s[i % 2], FFN_PARTS[i],
                                    ready=("g_lo", _F0[i]) if j == 0 else None)
                pe.wait_ge(S["acc_done"], 4 * KT)
                sums(("nm", 3), acc)

                for j in range(KT):
                    project(("pleg", j), ("pleg", j), xn, KT, ready=("xn_lo", 2 * KT) if j == 0 else None)
                    if j == 0:
                        pe.wait_ge(S["p_lo"], PLE // P)
                    project(("plep", j), ("plep", j), p_s, PLE // P)

            st.close()
            for sem in list(S.values()) + raw_in:
                nc.gpsimd.sem_clear(sem)
            nc.all_engine_barrier()

        with ExitStack() as st:
            y_st = st.enter_context(nc.semaphore("y_st"))
            block = st.enter_context(nc.Block())

            @block.sync
            def _(sp_):
                sp_.dma_start(y_out.rearrange("(k p) t -> p k t", p=P), xT[:]).then_inc(y_st, 16)
                sp_.wait_ge(y_st, 16)


def _shape_constants():
    c = np.zeros((P, NCONST), np.float32)
    k, q = np.arange(P)[:, None], np.arange(P)[None, :]
    c[:, C_ONES:C_ONES + P] = 1.0
    c[:, C_ID:C_ID + P] = np.eye(P)
    c[:, C_TRI:C_TRI + P] = np.where(k >= q, -1.0, 0.0)
    c[:, C_NEG1:C_NEG1 + P] = -1.0
    c[:, C_MD:C_MD + P] = np.where(k < q, 0.0, NEG)
    new = k - (P - DEC)
    one = np.where((new >= 0) & (new < np.arange(DEC)[None, :]), 0.0, NEG)
    c[:, C_MS:C_MS + 2 * P] = np.tile(one, (1, SH))
    c[:, C_MM:C_MM + P] = np.where((q // CHUNK) <= (k // CHUNK), 0.0, NEG)
    c[:, C_MT:C_MT + P] = np.where(q >= P - DEC, 0.0, NEG) + 0.0 * k
    half = ROPE // 2
    freqs = np.power(np.float32(10000.0), -np.arange(half, dtype=np.float32) / np.float32(half)).astype(np.float32)
    pos = np.concatenate([np.arange(SEQ), PAST + np.arange(DEC)]).astype(np.float32)
    ang = (pos[None, :] * freqs[:, None]).astype(np.float32)
    cs, sn = np.cos(ang), np.sin(ang)
    trig = np.concatenate([np.tile(np.concatenate([cs, cs]), (4, 1)),
                           np.tile(np.concatenate([-sn, sn]), (4, 1))], axis=1).astype(np.float32)
    return c, trig


def _stream(w):
    win = w["w_in"]
    at = dict(zip(("q", "k", "v", "m", "c", "r", "ga", "gb"),
                  np.cumsum([0, 512, 512, 512, MH * (NOPE + ROPE), LORA, ROPE, D]).tolist()))
    m = win[:, at["m"]:at["c"]].reshape(D, MH, NOPE + ROPE)

    def tiles(cols):
        nk = cols.shape[0] // P
        return cols.reshape(nk, P, -1).transpose(1, 0, 2).reshape(P, -1)

    out = np.zeros((len(CHUNKS), P, CW), np.float32)
    for n, c in enumerate(CHUNKS):
        kind, i = c[0], c[1]
        if kind == "v":
            a = tiles(win[2 * i * P:2 * (i + 1) * P, at["v"]:at["v"] + 512])
        elif kind in ("q", "k", "ga", "gb"):
            a = tiles(win[:, at[kind] + i * P:at[kind] + (i + 1) * P])
        elif kind == "c":
            a = tiles(win[:, at["c"]:at["r"]])
        elif kind == "kr":
            a = tiles(np.tile(win[:, at["r"]:at["ga"]], (1, 4)))
        elif kind == "qr":
            a = tiles(m[:, 4 * i:4 * i + 4, NOPE:].reshape(D, P))
        elif kind == "qn":
            a = tiles(m[:, 2 * i:2 * i + 2, :NOPE].reshape(D, P))
        elif kind == "ukuv":
            uk = w["w_uk"].reshape(LORA, PAIRS, 2 * NOPE).transpose(2, 1, 0).reshape(P, PAIRS * LORA)
            a = np.concatenate([uk, w["w_uv"].reshape(LORA, MH * MV)], axis=1)
        elif kind == "proj":
            a = np.concatenate([tiles(w["w_proj_sb"][:, i * P:(i + 1) * P]),
                                tiles(w["w_proj_mla"][:, i * P:(i + 1) * P])], axis=1)
        elif kind == "out":
            a = tiles(w["w_out"][:, i * P:(i + 1) * P])
        elif kind in ("upg", "upv"):
            f = i + FT * (kind == "upv")
            a = tiles(w["w_up"][:, f * P:(f + 1) * P])
        elif kind == "down":
            j = c[2]
            a = tiles(w["w_down"][_F0[i] * P:_F0[i + 1] * P, j * P:(j + 1) * P])
        elif kind == "pleg":
            a = tiles(w["w_ple_gate"][:, i * P:(i + 1) * P])
        else:
            a = tiles(w["w_ple_proj"][:, i * P:(i + 1) * P])
        out[n, :, :a.shape[1]] = a
    return out


_W = ("w_in", "w_uk", "w_uv", "w_proj_sb", "w_proj_mla", "w_out", "w_up", "w_down", "w_ple_gate", "w_ple_proj")


def _feature_major(rows):
    return rows.reshape(-1, P).T


def kernel(**inputs):
    import concourse.bacc as bacc
    from concourse.bass_utils import run_bass_kernel_spmd

    a = {n: np.asarray(x) for n, x in inputs.items()}
    consts, trig = _shape_constants()
    vecs = []
    for l in range(DEPTH):
        state = a["state_ffn_conv"][l, 0].reshape(2, 2 * FT, P).transpose(2, 1, 0).reshape(P, -1)
        parts = [_feature_major(a[n][l]) for n in ("g_pre_mix", "g_post_mix", "g_pre_ffn", "g_post_ffn",
                                                    "conv_w", "conv_b", "ckv_gain")]
        vecs.append(np.concatenate(parts + [state, np.zeros((P, 1), np.float32)], axis=1))
    blocks = lambda x: x.reshape(DEPTH, CB, P, -1)
    kcache = blocks(a["cache_sb_k"]).reshape(DEPTH, CB, P, PAIRS, P).transpose(0, 1, 4, 3, 2)
    rk = a["cache_mla_krope"][:, 0].transpose(0, 2, 1)
    ins = {
        "x_in": np.concatenate([a["x_prompt"][0], a["x_sample"][0]]).T,
        "p_in": np.concatenate([a["p_prompt"][:, 0], a["p_sample"][:, 0]], axis=1).transpose(0, 2, 1),
        "wstream": np.stack([_stream({n: a[n][l] for n in _W}) for l in range(DEPTH)]),
        "vec": np.stack(vecs),
        "kc": kcache.reshape(DEPTH, CB, P, PAIRS * P),
        "vc": blocks(a["cache_sb_v"]),
        "cct": a["cache_mla_ckv"][:, 0].transpose(0, 2, 1),
        "cc": a["cache_mla_ckv"][:, 0].reshape(DEPTH, CB, P, LORA).transpose(0, 2, 1, 3).reshape(DEPTH, P, CB * LORA),
        "krc": np.tile(rk, (1, 4, 1)),
        "consts": consts,
        "trig": trig,
    }
    outs = {"y_out": (D, T), "k_out": (DEPTH, SH * SD, T), "v_out": (DEPTH, T, SH * SD), "c_out": (DEPTH, LORA, T),
            "kr_out": (DEPTH, ROPE, T), "conv_out": (DEPTH, P, 2 * FT, 4)}
    nc = bacc.Bacc("TRN2", target_bir_lowering=False, num_devices=1, dynamic_dma_scratch_size=1024)
    arrays, args = {}, []
    for name, x in ins.items():
        x = np.ascontiguousarray(x)
        arrays[f"in_{name}"] = x
        args.append(nc.dram_tensor(f"in_{name}", x.shape, mybir.dt.from_np(x.dtype), kind="ExternalInput").ap())
    for name, shape in outs.items():
        args.append(nc.dram_tensor(f"out_{name}", shape, F32, kind="ExternalOutput").ap())
    build(nc, *args)
    r = run_bass_kernel_spmd(nc, [arrays], core_ids=[0]).results[0]
    y = r["out_y_out"].T
    k = r["out_k_out"].transpose(0, 2, 1).reshape(DEPTH, 1, T, SH, SD)
    v = r["out_v_out"].reshape(DEPTH, 1, T, SH, SD)
    c = r["out_c_out"].transpose(0, 2, 1)[:, None]
    kr = r["out_kr_out"].transpose(0, 2, 1)[:, None]
    cv = r["out_conv_out"].transpose(0, 3, 2, 1).reshape(DEPTH, 1, 4, 2 * DFF)
    halves = []
    for lo, hi in ((0, SEQ), (SEQ, T)):
        halves.append([k[:, :, lo:hi], v[:, :, lo:hi], c[:, :, lo:hi], kr[:, :, lo:hi]])
    halves[0].append(cv[:, :, 0:2])
    halves[1].append(cv[:, :, 2:4])
    out = [y[None, 0:SEQ], y[None, SEQ:T]] + halves[0] + halves[1]
    return tuple(np.ascontiguousarray(x) for x in out)
```

```python
from contextlib import ExitStack

import concourse.bass as bass
import numpy as np
from concourse import mybir

F32 = mybir.dt.float32
F32R = mybir.dt.float32r
BF16 = mybir.dt.bfloat16
ALU = mybir.AluOpType
ACT = mybir.ActivationFunctionType

P = 128
DEPTH = 2
D = 1024
KT = D // P
SEQ, DEC, PAST = 512, 32, 1024
T = SEQ + DEC
HT = T // 2
QB = SEQ // P
CB = PAST // P
TAIL = T - P
SH, SD = 8, 64
MH, NOPE, ROPE, MV, LORA = 8, 64, 32, 64, 128
CHUNK = 64
DFF = 2816
FT = DFF // P
PLE = 256
EPS = 1e-6
SB_SCALE = SD ** -0.5
MLA_SCALE = (NOPE + ROPE) ** -0.5
NEG = -1e30
PAIRS = SH // 2
CW = KT * P
FFN_PARTS = [8, 8, 6]
RAW_SLOTS, W_SLOTS = 2, 3
RW = 24448

CHUNKS = [("v", i) for i in range(4)]
for _t in range(PAIRS):
    CHUNKS += [("q", _t), ("k", _t)]
CHUNKS += [("c", 0), ("kr", 0), ("qr", 0), ("qr", 1), ("qn", 0), ("ukuv", 0)]
CHUNKS += [("qn", t) for t in range(1, PAIRS)]
CHUNKS += [("ga", 0), ("gb", 0), ("ga", 1), ("gb", 1)]
for _j in range(KT):
    CHUNKS += [("proj", _j)]
    if _j + 2 < KT:
        CHUNKS += [("ga", _j + 2), ("gb", _j + 2)]
CHUNKS += [("out", j) for j in range(KT)]
_F0 = [sum(FFN_PARTS[:i]) for i in range(len(FFN_PARTS) + 1)]


def _up(i):
    return [c for j in range(_F0[i], _F0[i + 1]) for c in (("upg", j), ("upv", j))]


def _down(i):
    return [("down", i, j) for j in range(KT)]


CHUNKS += _up(0) + _up(1) + _down(0) + _up(2) + _down(1) + _down(2)
CHUNKS += [c for j in range(KT) for c in (("pleg", j), ("plep", j))]
CHUNK_AT = {c: n for n, c in enumerate(CHUNKS)}
RING = [c for c in CHUNKS if c[0] != "ukuv"]
RING_AT = {c: n for n, c in enumerate(RING)}


def chunk_floats(c):
    if c[0] == "down":
        return FFN_PARTS[c[1]] * P
    return PLE // P * P if c[0] == "plep" else CW


V_GPM, V_GQM, V_GPF, V_GQF = 0, KT, 2 * KT, 3 * KT
V_CW = 4 * KT
V_CB = V_CW + 3 * 2 * FT
V_CG = V_CB + 2 * FT
V_ST = V_CG + 1
NV = V_ST + 2 * 2 * FT + 1

C_ONES, C_ID, C_TRI, C_NEG1 = 0, P, 2 * P, 3 * P
C_MD, C_MS, C_MM, C_MT = 4 * P, 5 * P, 7 * P, 8 * P
NCONST = 9 * P


def _q_swap(n=32):
    return [(i + n // 2) % n for i in range(n)]


def build(nc, x_in, p_in, wstream, vec, kc, vc, cct, cc, krc, consts, trig,
          y_out, k_out, v_out, c_out, kr_out, conv_out):
    top = ExitStack()
    with top:
        def sb(name, shape, dt=F32, stack=top):
            return stack.enter_context(nc.sbuf_tensor(name, shape, dt))

        ps = top.enter_context(nc.psum_tensor("ps", [P, 8, 512], F32))
        xT = sb("xT", [P, KT, T])
        con = sb("con", [P, NCONST - 2 * P])
        ones = con[:, C_ONES:C_ONES + P]
        ident = con[:, C_ID:C_ID + P]
        exact = sb("exact", [P, 2, P], F32R)
        masks = sb("masks", [P, 6, P], BF16)
        epsb = sb("epsb", [P, 1])
        ident_b = masks[:, 0]

        raw = sb("raw", [P, RAW_SLOTS, CW])
        wsp = sb("wsp", [P, W_SLOTS, 2, CW], F32R)
        xn = sb("xn", [P, 2, KT, T], F32R)
        R = sb("R", [P, RW], F32R)
        A = sb("A", [P, KT * T])
        mix = sb("mix", [P, 6, T + 4])
        rstd = sb("rstd", [P, T])
        acc = sb("acc", [P, T])
        vv = sb("vv", [P, NV])
        small = sb("small", [P, 8])
        ctail = sb("ctail", [P, 2 * FT, 4])

        fT = A[:, :].rearrange("p (k t) -> p k t", t=T)

        def reg(off, *dims):
            n = int(np.prod(dims))
            assert off + n <= RW, (off, n)
            ap = R[:, off:off + n]
            if len(dims) == 1:
                return ap
            names = "abcd"[:len(dims)]
            s = {names[i]: dims[i] for i in range(1, len(dims))}
            return ap.rearrange(f"p ({' '.join(names)}) -> p {' '.join(names)}", **s)

        o_sb = reg(0, 2, PAIRS, T)
        b = 2 * PAIRS * T
        v_s = reg(b, 2, QB + 1, SH * SD)
        b1 = b + 2 * (QB + 1) * SH * SD
        qk = reg(b1, 2, 2, 2, T)
        kcs = reg(b1 + 4 * T, 2, 2, PAIRS * P)
        b2 = b1 + 8 * T
        SPW = sum(SEQ - kb * P for kb in range(QB))
        sp = reg(b2, 2, 2 * SPW)
        b3 = b2 + 4 * SPW
        att = reg(b3, 2, 2, 512)
        b4 = b3 + 2048
        k_tail = reg(b4, 2, PAIRS, P)
        q_smp = reg(b4 + 2 * PAIRS * P, 2, PAIRS, 2 * DEC)
        qr = reg(b1, 2, 2, T)
        krT = reg(RW - 2 * T - 4 * P, 2, T)
        qr_smp = reg(RW - 4 * P, 2, 2, P)
        o_ml = reg(b, 2, PAIRS, T)
        ql_smp = reg(b + 2 * PAIRS * T, 2, MH, DEC)
        m0 = b1 + 4 * T
        cT = reg(m0, 2, T)
        ctok = reg(m0 + 2 * T, 2, QB + 1, P)
        m1 = m0 + 2 * T + 2 * (QB + 1) * P
        ukuv = reg(m1, 2, CW)
        m3 = m1 + 2 * CW
        qn = reg(m3, 2, T)
        ql = reg(m3 + 2 * T, 2, SEQ)
        m4 = m3 + 2 * T + 2 * SEQ
        PTS = 384
        PTW = 3 * PTS + 512
        pT = reg(m4, 2, PTW)
        ol = reg(m4 + 2 * PTW, 2, SEQ)
        assert m4 + 2 * PTW + 2 * SEQ <= RW - 2 * T - 4 * P
        cache_s = [reg(b1, 2, PAST), reg(m3, 2, PAST)]
        pT_s = reg(m3 + 2 * PAST, 2, CB + 1, 2 * P)
        assert m3 + 2 * PAST + 4 * (CB + 1) * P <= RW - 2 * T - 4 * P
        ol_s = reg(b1 + PAST, 2, 2 * P)
        mixin = reg(b + 2 * PAIRS * T, 2, KT, T)
        g_s = [reg(0, 2, 8, T), reg(16 * T, 2, 8, T)]
        p_s = reg(32 * T, 2, 2, T)

        tsp = A[:, 0:1024].rearrange("p (s n) -> p s n", n=512)
        araw = A[:, 1024:2048].rearrange("p (s n) -> p s n", n=512)
        kraw = A[:, 2048:2048 + T]
        vraw = A[:, 2592:2592 + 1024].rearrange("p (s n) -> p s n", n=512)
        kcraw = [vraw[:, 0], vraw[:, 1]]
        vcraw = [A[:, 2048:2560], A[:, 3616:4128]]
        craws = A[:, 0:2 * PAST].rearrange("p (k n) -> p k n", n=PAST)
        prw = A[:, 2 * PAST:2 * PAST + 1024].rearrange("p (s n) -> p s n", n=512)
        psm = A[:, 3072:3072 + (CB + 1) * P]
        rsum, negmax = small[:, 0:2], small[:, 2:4]
        cos, sin = mix[:, 0, 0:T], mix[:, 1, 0:T]
        sq = [mix[:, 2, 0:T], mix[:, 3, 0:T]]
        tmp = [mix[:, 4, 0:T], mix[:, 5, 0:T]]
        craw, rope = acc[:, :], tmp
        uext = [mix[:, 0], mix[:, 1]]
        uc = [mix[:, 2, 0:T + 2], mix[:, 3, 0:T + 2]]
        gel = mix[:, 4, 0:T + 2]
        gt = mix[:, 5, 0:T]

        def halves(ap):
            return ap.rearrange("p (h n) -> p h n", h=2)

        def ptile(n):
            return ps[:, 2 * (n % 2):2 * (n % 2) + 2, 0:HT]

        ZB, OB = 4, 7
        TB = 6
        s_view = ps[:, ZB:ZB + 3].rearrange("p b n -> p (b n)")[:, 0:(CB + 1) * P]

        def pt_view(x, qb):
            o = m4 + x * PTW + qb * P
            return R[:, o:o + PTS * (qb + 1)].rearrange("p (b q) -> p b q", q=PTS)[:, :, 0:P]

        with ExitStack() as st:
            pre = {n: st.enter_context(nc.semaphore(n)) for n in
                   ("con_in", "late_in", "x_in0", "x_in1", "x_in2", "x_in3", "made", "eps_made", "squares", "summed", "logs", "roots")}
            late = sb("late", [P, 2 * P])
            block = st.enter_context(nc.Block())
            XL = KT // 4

            @block.sync
            def _(sp_):
                sp_.dma_start(con[:], consts[:, 0:NCONST - 2 * P]).then_inc(pre["con_in"], 16)
                for i in range(4):
                    sp_.dma_start(xT[:, XL * i:XL * (i + 1)],
                                  x_in[XL * i * P:XL * (i + 1) * P].rearrange("(k p) t -> p k t", p=P)).then_inc(pre[f"x_in{i}"], 16)
                sp_.dma_start(late[:], consts[:, NCONST - 2 * P:]).then_inc(pre["late_in"], 16)

            @block.vector
            def _(dve):
                nc.vector.memset(epsb[:], EPS).then_inc(pre["eps_made"], 1)
                dve.wait_ge(pre["con_in"], 16)
                nc.vector.tensor_copy(exact[:, 0], con[:, C_TRI:C_TRI + P]).then_inc(pre["made"], 1)
                nc.vector.tensor_copy(exact[:, 1], con[:, C_NEG1:C_NEG1 + P]).then_inc(pre["made"], 1)
                nc.vector.tensor_copy(masks[:, 0], ident).then_inc(pre["made"], 1)
                nc.vector.tensor_copy(masks[:, 1:4].rearrange("p a b -> p (a b)"), con[:, C_MD:C_MD + 3 * P]).then_inc(pre["made"], 1)
                dve.wait_ge(pre["late_in"], 16)
                nc.vector.tensor_copy(masks[:, 4:6].rearrange("p a b -> p (a b)"), late[:]).then_inc(pre["made"], 1)
                dve.wait_ge(pre["made"], 5)

            @block.scalar
            def _(act):
                nc.scalar.preload_act_table_set("natural_log_exp_and_others")
                for k in range(KT):
                    act.wait_ge(pre[f"x_in{k // XL}"], 16)
                    if k >= 2:
                        act.wait_ge(pre["summed"], k - 1)
                    nc.scalar.activation(sq[k % 2], xT[:, k], ACT.Square).then_inc(pre["squares"], 1)
                act.wait_ge(pre["eps_made"], 1)
                act.wait_ge(pre["summed"], KT)
                nc.scalar.activation(halves(rstd[:]), ps[:, 0:2, 0:HT], ACT.Ln, bias=epsb[:],
                                     scale=1.0 / D).then_inc(pre["logs"], 1)
                act.wait_ge(pre["logs"], 1)
                nc.scalar.activation(rstd[:], rstd[:], ACT.Exp, scale=-0.5).then_inc(pre["roots"], 1)
                act.wait_ge(pre["roots"], 1)

            @block.tensor
            def _(pe):
                pe.wait_ge(pre["con_in"], 16)
                for k in range(KT):
                    pe.wait_ge(pre["squares"], k + 1)
                    for h in range(2):
                        mm = pe.matmul(ps[:, h, 0:HT], ones, sq[k % 2][:, h * HT:(h + 1) * HT], start=(k == 0), stop=(k == KT - 1))
                    mm.then_inc(pre["summed"], 1)

        m_units = [(h, qb) for h in range(MH) for qb in range(QB)]
        NM = len(m_units)
        LAG_PT = 3
        M_STEPS = NM + LAG_PT + 1
        QN_STEPS = (5, 6)

        GA_STEPS = (NM, NM + 1)

        def m_tiles(s):
            out = []
            if s % (2 * QB) == QN_STEPS[1] and s // (2 * QB) + 1 < PAIRS:
                out.append(("qn", s // (2 * QB) + 1))
            if s % QB == QB - 1 and s + 1 < NM:
                out.append(("ql", (s + 1) // QB))
            if s == GA_STEPS[1]:
                out.append(("ga", 0))
            if s % QB == QB - 2 and s > QB:
                out.append(("ol", s // QB - 1))
            if s % QB == QB - 1 and s > QB:
                out.append(("uv", s // QB - 1))
            return out

        def m_evacuated(s):
            return [t for t in m_tiles(s - 1) if t[0] == "uv"] + [t for t in m_tiles(s) if t[0] != "uv"]

        PT = [("q", 0), ("k", 0)]
        for t in range(1, PAIRS):
            PT += [("q", t), ("k", t)]
        PT += [("c", 0), ("kr", 0), ("cn", 0), ("qr", 0), ("qr", 1), ("qn", 0), ("ct", 0), ("ql", 0)]
        for s in range(M_STEPS):
            PT += m_tiles(s)
        PT += [("gb", 0), ("ga", 1), ("gb", 1), ("uvs", 0)]
        for j in range(KT):
            PT += [("ya", j), ("yb", j)]
            if j + 2 < KT:
                PT += [("ga", j + 2), ("gb", j + 2)]
        PT += [("out", j) for j in range(KT)] + [("nm", 1), ("nm", 2)]
        PT += _up(0) + _up(1) + _down(0) + _up(2) + _down(1) + _down(2) + [("nm", 3)]
        for j in range(KT):
            PT += [("pleg", j), ("plep", j)]
        PT += [("nm", 0)]
        AT = {t: n for n, t in enumerate(PT)}
        assert len(AT) == len(PT)
        ACT_ONLY = {"c", "kr", "qr", "cn", "nm", "ga", "gb", "out", "upg", "upv", "pleg"}

        def readers(t):
            if t[0] in ("ya", "yb", "plep") or (t[0] == "down" and t[1] > 0):
                return 0, 1
            return (1, 0) if t[0] in ACT_ONLY or t[0] == "down" else (1, 1)

        act_upto, dve_upto = [0], [0]
        for t in PT:
            act_upto.append(act_upto[-1] + readers(t)[0])
            dve_upto.append(dve_upto[-1] + readers(t)[1])

        def aread(t):
            return act_upto[AT[t] + 1]

        def dread(t):
            return dve_upto[AT[t] + 1]

        def last_tile(c):
            if c[0] == "proj":
                return ("yb", c[1])
            return c

        units = [("p", h, kb) for h in range(SH) for kb in reversed(range(QB))]
        units += [("s", 0, kb) for kb in reversed(range(CB + 1))]
        NU, NPU = len(units), SH * QB
        FIRST_CACHE = NPU + 1
        LAG_CUM, LAG_PV = 2, 3
        NSTEP = NU + LAG_PV + 1
        beside = []
        for t in range(1, PAIRS):
            s0 = (t - 1) * 2 * QB
            beside += [(("q", t), s0 + 1, s0 + 2, s0 + 4), (("k", t), s0 + 4, s0 + 5, s0 + 6)]
        beside += [(("c", 0), 25, 28, 29), (("kr", 0), 30, 32, 33), (("qr", 0), 34, 36, 36), (("qr", 1), 37, 38, 38),
                   (("qn", 0), 40, 42, NSTEP)]
        fill, out_in = {}, {}
        for t, f0, f1, e in beside:
            fill.setdefault(f0, []).append((t, 0))
            fill.setdefault(f1, []).append((t, 1))
            out_in.setdefault(e, []).append(t)
        CN_STEP = 34

        def width(u):
            return SEQ - P * u[2] if u[0] == "p" else MH * DEC

        def sp_off(u):
            if u[0] == "p":
                return (u[1] % 2) * SPW + sum(SEQ - P * k for k in range(u[2] + 1, QB))
            return (CB - u[2]) * SH * DEC

        def head_end(s):
            u = s - 1 - LAG_PV
            if 0 <= u < NPU and u % QB == QB - 1:
                return u // QB
            return SH if u == NU - 1 else None

        names = ("w_hi w_lo p_done act_read dve_read vec_in trig_in act_step dve_step "
                 "sq_done acc_done rstd_done norm_done xn_hi xn_lo r_mul x_even x_odd x_new sq2_done sq2_sum zeroed "
                 "v_chunk v_raw v_hi v_lo v_st0 v_st1 k_raw k_st "
                 "z_done t_abs t_exp t_ln sp_raw sp_hi sp_lo cum_done a_raw a_hi a_lo pv_done o_hi o_lo "
                 "kc_in0 kc_in1 vc_in0 vc_in1 kc_hi kc_lo vc_hi vc_lo "
                 "c_raw c_ready c_hi c_lo c_st rope_done rope_hi rope_lo kr_st "
                 "s_done m_neg e_done p_scaled tr_done pt_hi pt_lo sig0 "
                 "cs_in cs_hi cs_lo cc_in cc_hi cc_lo "
                 "ss_done ss_neg se_done ps_scaled str_done spt_hi spt_lo ols_mm ols_hi ols_lo "
                 "mi_raw mi_hi mi_lo f_raw conv0 conv2 gelu_done g_raw g_hi g_lo "
                 "p_in p_hi p_lo conv_st").split()

        with nc.Fori(0, DEPTH) as layer, ExitStack() as st:
            S = {n: st.enter_context(nc.semaphore(n)) for n in names}
            raw_in = [st.enter_context(nc.semaphore(f"raw_in{i}")) for i in range(RAW_SLOTS)]
            block = st.enter_context(nc.Block())

            @block.sync
            def _(sp_):
                state = [0]

                def load_to(n):
                    while state[0] < n:
                        c = state[0]
                        w = chunk_floats(CHUNKS[c])
                        if c >= RAW_SLOTS:
                            sp_.wait_ge(S["w_lo"], c - RAW_SLOTS + 1)
                        sp_.dma_start(raw[:, c % RAW_SLOTS, 0:w],
                                      wstream[layer, c, :, 0:w]).then_inc(raw_in[c % RAW_SLOTS], 16)
                        state[0] += 1

                sp_.dma_start(vv[:], vec[layer]).then_inc(S["vec_in"], 16)
                load_to(RAW_SLOTS)
                sp_.dma_start(mix[:, 0:2, 0:T], trig.rearrange("p (a t) -> p a t", a=2)).then_inc(S["trig_in"], 16)
                load_to(CHUNK_AT[("c", 0)] + 3)

                def load_k(i):
                    if i == 0:
                        sp_.wait_ge(S["v_st0"], 16 * ((QB + 2) // 2))
                        sp_.wait_ge(S["v_st1"], 16 * ((QB + 1) // 2))
                    if i >= 2:
                        sp_.wait_ge(S["kc_lo"], i - 1)
                    sp_.dma_start(kcraw[i % 2], kc[layer, CB - 1 - i]).then_inc(S[f"kc_in{i % 2}"], 16)

                def load_v(i):
                    if i == 0:
                        sp_.wait_ge(S["k_st"], 16 * PAIRS)
                    if i >= 2:
                        sp_.wait_ge(S["vc_lo"], i - 1)
                    sp_.dma_start(vcraw[i % 2], vc[layer, CB - 1 - i]).then_inc(S[f"vc_in{i % 2}"], 16)

                for load, i in ((load_k, 0), (load_k, 1), (load_v, 0), (load_v, 1), (load_to, CHUNK_AT[("qr", 1)] + 1),
                                (load_k, 2), (load_k, 3), (load_to, CHUNK_AT[("qn", 0)] + 1), (load_k, 4), (load_k, 5),
                                (load_v, 2), (load_k, 6), (load_v, 3), (load_to, CHUNK_AT[("ukuv", 0)] + 1),
                                (load_k, 7), (load_v, 4), (load_v, 5), (load_to, CHUNK_AT[("qn", 1)] + 1),
                                (load_v, 6), (load_v, 7)):
                    load(i)

                sp_.wait_ge(S["sp_lo"], NU)
                sp_.wait_ge(S["a_lo"], NU)
                sp_.dma_start(craws[:, 0], cct[layer]).then_inc(S["cs_in"], 16)
                sp_.dma_start(craws[:, 1], krc[layer]).then_inc(S["cs_in"], 16)
                load_to(CHUNK_AT[("ga", 0)] + RAW_SLOTS)
                sp_.wait_ge(S["cs_lo"], 1)
                sp_.dma_start(craws[:, 0], cc[layer]).then_inc(S["cc_in"], 16)
                load_to(CHUNK_AT[("down", len(FFN_PARTS) - 1, 2)])
                sp_.wait_ge(S["conv2"], 2 * FT)
                sp_.dma_start(mix[:, 0:2, 0:T], p_in[layer].rearrange("(k p) t -> p k t", p=P)).then_inc(S["p_in"], 16)
                sp_.wait_ge(S["act_read"], aread(("upv", FT - 1)))
                sp_.dma_start(conv_out[layer], ctail[:]).then_inc(S["conv_st"], 16)
                load_to(len(CHUNKS))
                sp_.wait_ge(S["conv_st"], 16)

            @block.gpsimd
            def _(pool):
                for c, ch in enumerate(CHUNKS):
                    w = chunk_floats(ch)
                    dst = ukuv if ch[0] == "ukuv" else wsp[:, RING_AT[ch] % W_SLOTS]
                    pool.wait_ge(S["w_hi"], c + 1)
                    nc.gpsimd.tensor_tensor(dst[:, 1, 0:w], raw[:, c % RAW_SLOTS, 0:w], dst[:, 0, 0:w].bitcast(F32),
                                            ALU.subtract).then_inc(S["w_lo"], 1)
                    if ch in (("upg", 0), ("pleg", 0)):
                        n0 = 0 if ch[0] == "upg" else KT
                        for j in range(1, KT, 2):
                            pool.wait_ge(S["r_mul"], n0 + j + 1)
                            nc.gpsimd.tensor_tensor(xT[:, j], xT[:, j], tmp[1], ALU.add).then_inc(S["x_odd"], 1)

            @block.scalar
            def _(act):
                ac = nc.scalar.activation
                split = [0]

                def split_to(n):
                    while split[0] <= min(n, len(CHUNKS) - 1):
                        c = split[0]
                        ch = CHUNKS[c]
                        w = chunk_floats(ch)
                        act.wait_ge(raw_in[c % RAW_SLOTS], 16 * (c // RAW_SLOTS + 1))
                        dst = ukuv if ch[0] == "ukuv" else wsp[:, RING_AT[ch] % W_SLOTS]
                        if ch[0] != "ukuv" and RING_AT[ch] >= W_SLOTS:
                            old = RING[RING_AT[ch] - W_SLOTS]
                            if old[0] == "v":
                                act.wait_ge(S["v_chunk"], old[1] + 1)
                            else:
                                act.wait_ge(S["p_done"], AT[last_tile(old)] + 1)
                        ac(dst[:, 0, 0:w], raw[:, c % RAW_SLOTS, 0:w], ACT.Copy).then_inc(S["w_hi"], 1)
                        split[0] += 1

                def tile(t, chunk=None):
                    if chunk is not None:
                        split_to(CHUNK_AT[chunk] + 1)
                    act.wait_ge(S["p_done"], AT[t] + 1)
                    return ptile(AT[t])

                def bank(t):
                    act.wait_ge(S["p_done"], AT[t] + 1)
                    return ps[:, 2 * (AT[t] % 2)]

                def rsqrt(t, n):
                    z = tile(t)
                    ac(halves(rstd[:]), z, ACT.Ln, bias=epsb[:], scale=1.0 / n).then_inc(S["act_read"], 1)
                    act.wait_ge(S["act_read"], aread(t))
                    ac(rstd[:], rstd[:], ACT.Exp, scale=-0.5).then_inc(S["rstd_done"], 1)

                def square(n, src, sem="sq_done"):
                    if n >= 2:
                        act.wait_ge(S["acc_done"], n - 1)
                    ac(sq[n % 2] if src.ndim == 2 else halves(sq[n % 2]), src, ACT.Square).then_inc(S[sem], 1)

                def xn_hi(n0, j, src):
                    act.wait_ge(S["norm_done"], n0 + j + 1)
                    ac(xn[:, 0, j], src, ACT.Copy).then_inc(S["xn_hi"], 1)

                def x_ready(n0, j):
                    act.wait_ge(S["x_odd" if j % 2 else "x_even"], (n0 + j) // 2 + 1)

                for j in range(KT):
                    xn_hi(0, j, tmp[j % 2])
                    if j in (0, 2):
                        split_to(j // 2)

                split_to(5)
                act.wait_ge(S["v_chunk"], 4)
                for i in range(QB + 1):
                    if i >= 2:
                        act.wait_ge(S[f"v_st{i % 2}"], 16 * (i // 2))
                    ac(vraw[:, i % 2], ps[:, 3 + i], ACT.Copy).then_inc(S["v_raw"], 1)
                    ac(v_s[:, 0, i], ps[:, 3 + i], ACT.Copy).then_inc(S["v_hi"], 1)
                    act.wait_ge(S["v_raw"], i + 1)
                    if i < QB:
                        act.dma_start(v_out[layer, i * P:(i + 1) * P], vraw[:, i % 2]).then_inc(S[f"v_st{i % 2}"], 16)
                    else:
                        act.dma_start(v_out[layer, SEQ:T], vraw[P - DEC:P, i % 2]).then_inc(S[f"v_st{i % 2}"], 16)

                def qk_tile(t):
                    z = tile(t, t if t[1] == 0 else None)
                    n = t[1]
                    if t[0] == "q":
                        for r in range(2):
                            ac(q_smp[64 * r:64 * r + 64, 0, n, DEC * r:DEC * r + DEC],
                               z[64 * r:64 * r + 64, 1, HT - DEC:HT], ACT.Copy, scale=SB_SCALE)
                        ac(halves(qk[:, n % 2, 0, 0]), z, ACT.Copy, scale=SB_SCALE).then_inc(S["act_read"], 1)
                    else:
                        if n > 0:
                            act.wait_ge(S["k_st"], 16 * n)
                        ac(halves(kraw), z, ACT.Copy).then_inc(S["k_raw"], 1)
                        ac(k_tail[:, 0, n], z[:, 1, HT - P:HT], ACT.Copy)
                        ac(halves(qk[:, n % 2, 1, 0]), z, ACT.Copy).then_inc(S["act_read"], 1)
                        act.wait_ge(S["k_raw"], n + 1)
                        act.dma_start(k_out[layer, n * P:(n + 1) * P], kraw).then_inc(S["k_st"], 16)

                act.wait_ge(S["zeroed"], 2)
                qk_tile(("q", 0))
                qk_tile(("k", 0))

                def c_tile():
                    z = tile(("c", 0), ("c", 0))
                    ac(halves(craw), z, ACT.Copy).then_inc(S["c_raw"], 1)
                    ac(halves(sq[0]), z, ACT.Square).then_inc(S["act_read"], 1)

                def rope_raw(n, t):
                    z = tile(t, t)
                    if n > 0:
                        act.wait_ge(S["rope_lo"], n)
                    if n == 1:
                        act.wait_ge(S["kr_st"], 16)
                    ac(halves(rope[0]), z, ACT.Copy).then_inc(S["act_read"], 1)

                def rope_parts(n):
                    act.wait_ge(S["rope_done"], n + 1)
                    if n == 0:
                        act.dma_start(kr_out[layer], rope[0][0:ROPE]).then_inc(S["kr_st"], 16)
                        ac(krT[:, 0], rope[0], ACT.Copy).then_inc(S["rope_hi"], 1)
                    else:
                        if n == 1:
                            act.wait_ge(S["z_done"], (PAIRS - 1) * 2 * QB)
                        for a in range(4):
                            ac(qr_smp[32 * a:32 * a + 32, 0, n - 1, DEC * a:DEC * a + DEC],
                               rope[0][32 * a:32 * a + 32, SEQ:T], ACT.Copy)
                        ac(qr[:, 0, n - 1], rope[0], ACT.Copy).then_inc(S["rope_hi"], 1)

                ROPES = {("kr", 0): 0, ("qr", 0): 1, ("qr", 1): 2}

                for s in range(NSTEP):
                    h = head_end(s)
                    if h is not None:
                        act.wait_ge(S["pv_done"], s - LAG_PV)
                        if h < SH:
                            r = 64 * (h % 2)
                            ac(o_sb[r:r + 64, 0, h // 2, 0:SEQ], ps[r:r + 64, OB], ACT.Copy).then_inc(S["o_hi"], 1)
                        else:
                            for r in range(2):
                                ins = ac(o_sb[64 * r:64 * r + 64, 0, :, SEQ:T],
                                         ps[64 * r:64 * r + 64, OB, 0:MH * DEC]
                                         .rearrange("p (t c) -> p t c", t=PAIRS)[:, :, DEC * r:DEC * r + DEC], ACT.Copy)
                            ins.then_inc(S["o_hi"], 1)
                    i = s + 1 - FIRST_CACHE
                    if 0 <= i < CB:
                        act.wait_ge(S[f"kc_in{i % 2}"], 16 * (i // 2 + 1))
                        act.wait_ge(S["z_done"], max(NPU, FIRST_CACHE + i - 1))
                        ac(kcs[:, 0, i % 2], kcraw[i % 2], ACT.Copy).then_inc(S["kc_hi"], 1)
                    i = s + 1 - FIRST_CACHE - LAG_PV
                    if 0 <= i < CB:
                        act.wait_ge(S[f"vc_in{i % 2}"], 16 * (i // 2 + 1))
                        act.wait_ge(S["pv_done"], max(NPU, FIRST_CACHE + i - 3))
                        ac(v_s[:, 0, i % 4], vcraw[i % 2], ACT.Copy).then_inc(S["vc_hi"], 1)
                    if s < NU:
                        w = width(units[s])
                        act.wait_ge(S["z_done"], s + 1)
                        if s >= 2:
                            act.wait_ge(S["sp_lo"], s - 1)
                        ac(tsp[:, s % 2, 0:w], ps[:, ZB + s % 3, 0:w], ACT.Abs).then_inc(S["t_abs"], 1)
                        act.wait_ge(S["t_abs"], s + 1)
                        ac(tsp[:, s % 2, 0:w], tsp[:, s % 2, 0:w], ACT.Exp, scale=-1.0).then_inc(S["t_exp"], 1)
                    if 1 <= s <= NU:
                        u, n = units[s - 1], s - 1
                        w1, o = width(u), sp_off(u)
                        act.wait_ge(S["sp_raw"], s)
                        if n >= 4:
                            act.wait_ge(S["cum_done"], n - 3)
                        ac(sp[:, 0, o:o + w1], tsp[:, n % 2, 0:w1], ACT.Copy).then_inc(S["sp_hi"], 1)
                    n = s - LAG_CUM
                    if 0 <= n < NU:
                        w2 = width(units[n])
                        act.wait_ge(S["cum_done"], n + 1)
                        if n >= 2:
                            act.wait_ge(S["a_lo"], n - 1)
                        ac(araw[:, n % 2, 0:w2], ps[:, ZB + n % 3, 0:w2], ACT.Exp).then_inc(S["a_raw"], 1)
                    if s < NU:
                        act.wait_ge(S["t_exp"], s + 1)
                        ac(tsp[:, s % 2, 0:w], tsp[:, s % 2, 0:w], ACT.Ln, bias=1.0).then_inc(S["t_ln"], 1)
                    for t in out_in.get(s - 1, []):
                        if t in ROPES:
                            rope_parts(ROPES[t])
                    for t in out_in.get(s, []):
                        if t[0] in ("q", "k"):
                            qk_tile(t)
                        elif t[0] == "c":
                            c_tile()
                        elif t in ROPES:
                            rope_raw(ROPES[t], t)
                    if s == CN_STEP:
                        rsqrt(("cn", 0), LORA)
                    for t, i in fill.get(s, []):
                        if i == 0 and t[0] != "qn":
                            split_to(CHUNK_AT[t] + 1)

                z = tile(("qn", 0), ("qn", 0))
                ac(halves(qn[:, 0]), z, ACT.Copy).then_inc(S["act_read"], 1)
                act.wait_ge(S["c_ready"], 1)
                act.dma_start(c_out[layer], craw).then_inc(S["c_st"], 16)
                ac(cT[:, 0], craw, ACT.Copy).then_inc(S["c_hi"], 1)
                n = AT[("ct", 0)]
                act.wait_ge(S["p_done"], n + 1)
                ac(ctok[:, 0, 0:QB], ps[:, 2 * (n % 2)].rearrange("p (b l) -> p b l", l=P), ACT.Copy)
                ac(ctok[:, 0, QB], ps[:, 2 * (n % 2) + 1, 0:P], ACT.Copy).then_inc(S["act_read"], 1)

                def gate(t, func):
                    z = tile(t, t)
                    ac(halves(mix[:, 2 * (t[0] == "gb") + t[1] % 2, 0:T]), z, func).then_inc(S["act_read"], 1)

                def m_tile(t):
                    if t[0] == "qn":
                        z = tile(t, t)
                        act.wait_ge(S["p_done"], AT[("ql", 2 * t[1] - 1)] + 1)
                        ac(halves(qn[:, 0]), z, ACT.Copy).then_inc(S["act_read"], 1)
                    elif t[0] == "ga":
                        gate(t, ACT.Copy)
                    elif t[0] == "ql":
                        z, h = bank(t), t[1]
                        if h > 0:
                            act.wait_ge(S["s_done"], QB * h)
                        ac(ql_smp[:, 0, h], ps[:, 2 * (AT[t] % 2) + 1, 0:DEC], ACT.Copy)
                        ac(ql[:, 0], z, ACT.Copy).then_inc(S["act_read"], 1)
                    elif t[0] == "ol":
                        z, h = bank(t), t[1]
                        if h > 0:
                            act.wait_ge(S["p_done"], AT[("uv", h - 1)] + 1)
                        ac(ol[:, 0], z, ACT.Copy).then_inc(S["act_read"], 1)
                    else:
                        z, r = bank(t), 64 * (t[1] % 2)
                        ac(o_ml[r:r + 64, 0, t[1] // 2, 0:SEQ], z[r:r + 64], ACT.Copy).then_inc(S["act_read"], 1)

                m_tile(("ql", 0))
                for s in range(M_STEPS):
                    n = s - LAG_PT
                    if 0 <= n < NM:
                        h, qb = m_units[n]
                        act.wait_ge(S["tr_done"], n + 1)
                        if h > 0:
                            act.wait_ge(S["p_done"], AT[("ol", h - 1)] + 1)
                        ac(pt_view(0, qb), ps[:, TB + n % 2, 0:P * (qb + 1)].rearrange("p (b q) -> p b q", q=P),
                           ACT.Copy).then_inc(S["pt_hi"], 1)
                    n = s - 1
                    if 0 <= n < NM:
                        w = P * (m_units[n][1] + 1)
                        act.wait_ge(S["m_neg"], n + 1)
                        if n >= 2:
                            act.wait_ge(S["tr_done"], n - 1)
                        ac(prw[:, n % 2, 0:w], ps[:, ZB + n % 2, 0:w], ACT.Exp, bias=negmax[:, n % 2:n % 2 + 1],
                           scale=MLA_SCALE, accum_out=rsum[:, n % 2:n % 2 + 1]).then_inc(S["e_done"], 1)
                    for t in m_evacuated(s):
                        m_tile(t)
                    if s == 1:
                        split_to(CHUNK_AT[("qn", 1)])
                m_tile(("uv", MH - 1))

                split_to(CHUNK_AT[("gb", 0)])
                act.wait_ge(S["cs_in"], 32)
                act.wait_ge(S["p_done"], AT[("uv", MH - 1)] + 1)
                ac(cache_s[0], craws, ACT.Copy).then_inc(S["cs_hi"], 1)
                for g in range(2):
                    act.wait_ge(S["ss_neg"], g + 1)
                    if g > 0:
                        act.wait_ge(S["str_done"], g)
                    ac(psm, s_view, ACT.Exp, bias=negmax[:, g:g + 1], scale=MLA_SCALE,
                       accum_out=rsum[:, g:g + 1]).then_inc(S["se_done"], 1)
                    gate((("gb", 0), ("ga", 1))[g], ACT.Copy)
                    if g == 1:
                        act.wait_ge(S["cc_in"], 16)
                        act.wait_ge(S["ss_done"], 2)
                        ac(cache_s[0][:, 0], craws[:, 0], ACT.Copy).then_inc(S["cc_hi"], 1)
                    act.wait_ge(S["str_done"], g + 1)
                    ac(pT_s[:, 0, :, g * P:(g + 1) * P], s_view.rearrange("p (b q) -> p b q", q=P),
                       ACT.Copy).then_inc(S["spt_hi"], 1)
                act.wait_ge(S["ols_mm"], 1)
                ac(ol_s[:, 0], ps[:, OB, 0:2 * P], ACT.Copy).then_inc(S["ols_hi"], 1)
                gate(("gb", 1), ACT.Sigmoid)
                z = bank(("uvs", 0))
                for r in range(2):
                    ins = ac(o_ml[64 * r:64 * r + 64, 0, :, SEQ:T],
                             z[64 * r:64 * r + 64, 0:MH * DEC]
                             .rearrange("p (t c) -> p t c", t=PAIRS)[:, :, DEC * r:DEC * r + DEC], ACT.Copy)
                ins.then_inc(S["act_read"], 1)
                act.wait_ge(S["act_read"], aread(("ga", 1)))
                for n in (0, 2, 1):
                    ac(mix[:, n, 0:T], mix[:, n, 0:T], ACT.Sigmoid).then_inc(S["sig0"], 1)

                for j in range(KT):
                    split_to(CHUNK_AT[("proj", j)] + 1)
                    act.wait_ge(S["mi_raw"], j + 1)
                    ac(mixin[:, 0, j], tmp[0], ACT.Copy).then_inc(S["mi_hi"], 1)
                    if j + 2 < KT:
                        act.wait_ge(S["dve_read"], dread(("yb", j)))
                        gate(("ga", j + 2), ACT.Sigmoid)
                        gate(("gb", j + 2), ACT.Sigmoid)

                for j in range(KT):
                    z = tile(("out", j), ("out", j))
                    ac(halves(fT[:, j]), z, ACT.Copy).then_inc(S["f_raw"], 1)
                    if j == 0:
                        act.wait_ge(S["dve_read"], dread(("yb", KT - 1)))
                    square(j, z, "act_read")
                nc.scalar.preload_act_table_set("natural_log_exp_and_others")
                rsqrt(("nm", 1), D)
                for j in range(KT):
                    x_ready(0, j)
                    if j >= 2:
                        act.wait_ge(S["sq2_sum"], j - 1)
                    ac(sq[j % 2], xT[:, j], ACT.Square).then_inc(S["sq2_done"], 1)
                rsqrt(("nm", 2), D)
                split_to(CHUNK_AT[("upv", 0)])
                for j in range(KT):
                    xn_hi(KT, j, tmp[j % 2])
                split_to(CHUNK_AT[("upg", 1)])

                def u_tile(t):
                    v, j = t[0] == "upv", t[1]
                    f, n = j + FT * v, 2 * j + v
                    z = tile(t, t)
                    e = uext[v]
                    if j > 0:
                        act.wait_ge(S["conv2"], n - 1)
                    ac(e[:, 2:2 + HT], z[:, 0], ACT.Copy)
                    ac(e[:, 2 + HT:2 + SEQ], z[:, 1, 0:SEQ - HT], ACT.Copy)
                    ac(e[:, 4 + SEQ:4 + T], z[:, 1, SEQ - HT:HT], ACT.Copy)
                    ac(e[:, 2 + SEQ:4 + SEQ], vv[:, V_ST + 2 * f:V_ST + 2 * f + 2], ACT.Copy)
                    b0 = 2 * (AT[t] % 2) + 1
                    ac(ctail[:, f].rearrange("p (a b) -> p a b", a=2),
                       ps[:, b0, SEQ - HT - 2:SEQ - HT - 2 + 2 * DEC].rearrange("p (a b) -> p a b", a=2)[:, :, 0:2],
                       ACT.Copy).then_inc(S["act_read"], 1)
                    act.wait_ge(S["act_read"], aread(t))
                    if v and j > 0:
                        act.wait_ge(S["g_raw"], j)
                    ac(uc[v], e[:, 0:T + 2], ACT.Identity, scale=vv[:, V_CW + f:V_CW + f + 1],
                       bias=vv[:, V_CB + f:V_CB + f + 1]).then_inc(S["conv0"], 1)

                def g_place(j):
                    i = 0 if j < _F0[1] else 1 if j < _F0[2] else 2
                    return i, g_s[i % 2], j - _F0[i]

                def g_high(j):
                    act.wait_ge(S["g_raw"], j + 1)
                    i, g, k = g_place(j)
                    if i == 2:
                        act.wait_ge(S["p_done"], AT[("down", 0, KT - 1)] + 1)
                    ac(g[:, 0, k], gt, ACT.Copy).then_inc(S["g_hi"], 1)

                act.wait_ge(S["zeroed"], 3)
                for part in (0, 1, "d0", 2, "d1", "d2"):
                    if part in (0, 1, 2):
                        for j in range(_F0[part], _F0[part + 1]):
                            u_tile(("upg", j))
                            if j > _F0[part]:
                                g_high(j - 1)
                            u_tile(("upv", j))
                            act.wait_ge(S["conv2"], 2 * j + 1)
                            ac(gel, uc[0], ACT.Gelu_apprx_tanh).then_inc(S["gelu_done"], 1)
                        split_to(CHUNK_AT[("upv", j)] + 2)
                        g_high(j)
                    elif part == "d0":
                        for j in range(KT):
                            z = tile(("down", 0, j), ("down", 0, j))
                            ac(halves(fT[:, j]), z, ACT.Copy).then_inc(S["act_read"], 1)
                    elif part == "d1":
                        for j in range(KT):
                            split_to(CHUNK_AT[("down", 1, j)] + 1)
                    else:
                        for j in range(KT):
                            split_to(CHUNK_AT[("down", 2, j)] + 1)
                            act.wait_ge(S["dve_read"], dread(("down", 2, j)))
                            square(KT + j, fT[:, j])
                nc.scalar.preload_act_table_set("natural_log_exp_and_others")
                act.wait_ge(S["p_in"], 16)
                for k in range(PLE // P):
                    ac(p_s[:, 0, k], mix[:, k, 0:T], ACT.Copy).then_inc(S["p_hi"], 1)
                rsqrt(("nm", 3), D)
                for j in range(KT):
                    x_ready(KT, j)
                    ac(xn[:, 0, j], xT[:, j], ACT.Copy).then_inc(S["xn_hi"], 1)

                for j in range(KT):
                    z = tile(("pleg", j), ("plep", j))
                    if j >= 2:
                        act.wait_ge(S["dve_read"], dread(("plep", j - 2)))
                    if j == 0:
                        act.wait_ge(S["p_lo"], PLE // P)
                    ac(halves(mix[:, j % 2, 0:T]), z, ACT.Sigmoid).then_inc(S["act_read"], 1)
                    if j > 0:
                        act.wait_ge(S["x_new"], j)
                        square(2 * KT + j - 1, xT[:, j - 1])
                nc.scalar.preload_act_table_set("natural_log_exp_and_others")
                act.wait_ge(S["x_new"], KT)
                square(3 * KT - 1, xT[:, KT - 1])
                rsqrt(("nm", 0), D)
                act.wait_ge(S["v_st0"], 16 * ((QB + 2) // 2))
                act.wait_ge(S["v_st1"], 16 * ((QB + 1) // 2))
                act.wait_ge(S["k_st"], 16 * PAIRS)
                act.wait_ge(S["c_st"], 16)
                act.wait_ge(S["kr_st"], 16)
                act.wait_ge(S["rstd_done"], 5)

            @block.vector
            def _(dve):
                v = nc.vector
                steps = [0]

                def link(ins):
                    steps[0] += 1
                    ins.then_inc(S["dve_step"], 1)
                    dve.wait_ge(S["dve_step"], steps[0])

                def lo(dst, src, hi, sem, scale=1.0):
                    ins = v.scalar_tensor_tensor(dst, src, scale, hi.bitcast(F32), ALU.mult, ALU.subtract)
                    if sem is not None:
                        ins.then_inc(S[sem], 1)

                def add_squares(n, sem, count):
                    dve.wait_ge(S[sem], count)
                    if n == 0:
                        dve.wait_ge(S["c_st"], 16)
                    if n % KT == 0:
                        v.tensor_copy(acc[:], sq[n % 2]).then_inc(S["acc_done"], 1)
                    else:
                        dve.wait_ge(S["acc_done"], n)
                        v.tensor_tensor(acc[:], acc[:], sq[n % 2], ALU.add).then_inc(S["acc_done"], 1)

                def normed(n0, gain, which):
                    if which is not None:
                        dve.wait_ge(S["rstd_done"], which)
                    for j in range(KT + 1):
                        if j < KT:
                            if j >= 2:
                                dve.wait_ge(S["xn_lo"], n0 + j - 1)
                            v.scalar_tensor_tensor(tmp[j % 2], xT[:, j], vv[:, gain + j:gain + j + 1], rstd[:],
                                                   ALU.mult, ALU.mult).then_inc(S["norm_done"], 1)
                        if j > 0:
                            dve.wait_ge(S["xn_hi"], n0 + j)
                            lo(xn[:, 1, j - 1], tmp[(j - 1) % 2], xn[:, 0, j - 1], "xn_lo")

                v.memset(q_smp.bitcast(F32), 0.0).then_inc(S["zeroed"], 1)
                v.memset(qr_smp.bitcast(F32), 0.0).then_inc(S["zeroed"], 1)
                dve.wait_ge(S["vec_in"], 16)
                normed(0, V_GPM, None)

                for i in range(QB + 1):
                    dve.wait_ge(S["v_hi"], i + 1)
                    lo(v_s[:, 1, i], ps[:, 3 + i], v_s[:, 0, i], "v_lo")

                def qk_tile(t):
                    n = t[1]
                    dve.wait_ge(S["act_read"], aread(t))
                    z = ptile(AT[t])
                    if t[0] == "q":
                        for r in range(2):
                            lo(q_smp[64 * r:64 * r + 64, 1, n, DEC * r:DEC * r + DEC],
                               z[64 * r:64 * r + 64, 1, HT - DEC:HT],
                               q_smp[64 * r:64 * r + 64, 0, n, DEC * r:DEC * r + DEC], None, SB_SCALE)
                        lo(halves(qk[:, n % 2, 0, 1]), z, halves(qk[:, n % 2, 0, 0]), "dve_read", SB_SCALE)
                    else:
                        lo(k_tail[:, 1, n], z[:, 1, HT - P:HT], k_tail[:, 0, n], None)
                        lo(halves(qk[:, n % 2, 1, 1]), z, halves(qk[:, n % 2, 1, 0]), "dve_read")

                qk_tile(("q", 0))
                qk_tile(("k", 0))

                def rope_rotate(n, t):
                    dve.wait_ge(S["act_read"], aread(t))
                    if n == 0:
                        dve.wait_ge(S["trig_in"], 16)
                    link(v.stream_shuffle(rope[1], rope[0], _q_swap()))
                    link(v.tensor_tensor(rope[1], rope[1], sin, ALU.mult))
                    link(v.tensor_tensor(rope[0], rope[0], cos, ALU.mult))
                    v.tensor_tensor(rope[0], rope[0], rope[1], ALU.add).then_inc(S["rope_done"], 1)

                def rope_low(n):
                    dve.wait_ge(S["rope_hi"], n + 1)
                    if n == 0:
                        lo(krT[:, 1], rope[0], krT[:, 0], "rope_lo")
                    else:
                        for a in range(4):
                            lo(qr_smp[32 * a:32 * a + 32, 1, n - 1, DEC * a:DEC * a + DEC],
                               rope[0][32 * a:32 * a + 32, SEQ:T],
                               qr_smp[32 * a:32 * a + 32, 0, n - 1, DEC * a:DEC * a + DEC], None)
                        lo(qr[:, 1, n - 1], rope[0], qr[:, 0, n - 1], "rope_lo")

                ROPES = {("kr", 0): 0, ("qr", 0): 1, ("qr", 1): 2}

                for s in range(NSTEP):
                    h = head_end(s)
                    if h is not None:
                        dve.wait_ge(S["o_hi"], h + 1)
                        if h < SH:
                            r = 64 * (h % 2)
                            lo(o_sb[r:r + 64, 1, h // 2, 0:SEQ], ps[r:r + 64, OB], o_sb[r:r + 64, 0, h // 2, 0:SEQ], "o_lo")
                        else:
                            for r in range(2):
                                lo(o_sb[64 * r:64 * r + 64, 1, :, SEQ:T],
                                   ps[64 * r:64 * r + 64, OB, 0:MH * DEC]
                                   .rearrange("p (t c) -> p t c", t=PAIRS)[:, :, DEC * r:DEC * r + DEC],
                                   o_sb[64 * r:64 * r + 64, 0, :, SEQ:T], "o_lo" if r else None)
                    i = s + 1 - FIRST_CACHE
                    if 0 <= i < CB:
                        dve.wait_ge(S["kc_hi"], i + 1)
                        lo(kcs[:, 1, i % 2], kcraw[i % 2], kcs[:, 0, i % 2], "kc_lo")
                    i = s + 1 - FIRST_CACHE - LAG_PV
                    if 0 <= i < CB:
                        dve.wait_ge(S["vc_hi"], i + 1)
                        lo(v_s[:, 1, i % 4], vcraw[i % 2], v_s[:, 0, i % 4], "vc_lo")
                    w = width(units[s]) if s < NU else 0
                    if 1 <= s <= NU:
                        u, n = units[s - 1], s - 1
                        w1, o = width(u), sp_off(u)
                        dve.wait_ge(S["sp_hi"], s)
                        lo(sp[:, 1, o:o + w1], tsp[:, n % 2, 0:w1], sp[:, 0, o:o + w1], "sp_lo")
                    n = s - LAG_CUM
                    if 0 <= n < NU:
                        w2 = width(units[n])
                        dve.wait_ge(S["a_raw"], n + 1)
                        if n >= 2:
                            dve.wait_ge(S["pv_done"], n - 1)
                        v.tensor_copy(att[:, n % 2, 0, 0:w2], araw[:, n % 2, 0:w2]).then_inc(S["a_hi"], 1)
                        dve.wait_ge(S["a_hi"], n + 1)
                        lo(att[:, n % 2, 1, 0:w2], araw[:, n % 2, 0:w2], att[:, n % 2, 0, 0:w2], "a_lo")
                    if s < NU:
                        dve.wait_ge(S["t_ln"], s + 1)
                        v.scalar_tensor_tensor(tsp[:, s % 2, 0:w], ps[:, ZB + s % 3, 0:w], 0.0, tsp[:, s % 2, 0:w],
                                               ALU.max, ALU.add).then_inc(S["sp_raw"], 1)
                    for t in out_in.get(s - 1, []):
                        if t in ROPES:
                            rope_low(ROPES[t])
                    for t in out_in.get(s, []):
                        if t[0] in ("q", "k"):
                            qk_tile(t)
                        elif t in ROPES:
                            rope_rotate(ROPES[t], t)
                    if s == CN_STEP:
                        dve.wait_ge(S["rstd_done"], 1)
                        v.scalar_tensor_tensor(craw, craw, vv[:, V_CG:V_CG + 1], rstd[:], ALU.mult,
                                               ALU.mult).then_inc(S["c_ready"], 1)

                dve.wait_ge(S["act_read"], aread(("qn", 0)))
                lo(halves(qn[:, 1]), ptile(AT[("qn", 0)]), halves(qn[:, 0]), "dve_read")
                dve.wait_ge(S["c_hi"], 1)
                lo(cT[:, 1], craw, cT[:, 0], "c_lo")
                dve.wait_ge(S["act_read"], aread(("ct", 0)))
                n = AT[("ct", 0)]
                lo(ctok[:, 1, 0:QB], ps[:, 2 * (n % 2)].rearrange("p (b l) -> p b l", l=P), ctok[:, 0, 0:QB], None)
                lo(ctok[:, 1, QB], ps[:, 2 * (n % 2) + 1, 0:P], ctok[:, 0, QB], "dve_read")

                def m_tile(t):
                    if t[0] == "ga":
                        return
                    dve.wait_ge(S["act_read"], aread(t))
                    z = ps[:, 2 * (AT[t] % 2)]
                    if t[0] == "qn":
                        lo(halves(qn[:, 1]), ptile(AT[t]), halves(qn[:, 0]), "dve_read")
                    elif t[0] == "ql":
                        h = t[1]
                        lo(ql_smp[:, 1, h], ps[:, 2 * (AT[t] % 2) + 1, 0:DEC], ql_smp[:, 0, h], None)
                        lo(ql[:, 1], z, ql[:, 0], "dve_read")
                    elif t[0] == "ol":
                        lo(ol[:, 1], z, ol[:, 0], "dve_read")
                    else:
                        r = 64 * (t[1] % 2)
                        lo(o_ml[r:r + 64, 1, t[1] // 2, 0:SEQ], z[r:r + 64], o_ml[r:r + 64, 0, t[1] // 2, 0:SEQ], "dve_read")

                m_tile(("ql", 0))
                for s in range(M_STEPS):
                    n = s - 1
                    if 0 <= n < NM:
                        i, w = n % 2, P * (m_units[n][1] + 1)
                        dve.wait_ge(S["s_done"], n + 1)
                        link(v.reduce_max(negmax[:, i:i + 1], ps[:, ZB + i, 0:w], mybir.AxisListType.X))
                        v.tensor_scalar(negmax[:, i:i + 1], negmax[:, i:i + 1], -MLA_SCALE, None,
                                        ALU.mult).then_inc(S["m_neg"], 1)
                    n2 = s - LAG_PT
                    if 0 <= n2 < NM:
                        qb = m_units[n2][1]
                        dve.wait_ge(S["pt_hi"], n2 + 1)
                        lo(pt_view(1, qb), ps[:, TB + n2 % 2, 0:P * (qb + 1)].rearrange("p (b q) -> p b q", q=P),
                           pt_view(0, qb), "pt_lo")
                    if 0 <= n < NM:
                        dve.wait_ge(S["e_done"], n + 1)
                        link(v.reciprocal(rsum[:, i:i + 1], rsum[:, i:i + 1]))
                        v.tensor_scalar(prw[:, i, 0:w], prw[:, i, 0:w], rsum[:, i:i + 1], None,
                                        ALU.mult).then_inc(S["p_scaled"], 1)
                    for t in m_evacuated(s):
                        m_tile(t)
                m_tile(("uv", MH - 1))

                dve.wait_ge(S["cs_hi"], 1)
                lo(cache_s[1], craws, cache_s[0], "cs_lo")
                for g in range(2):
                    dve.wait_ge(S["ss_done"], g + 1)
                    link(v.reduce_max(negmax[:, g:g + 1], s_view, mybir.AxisListType.X))
                    v.tensor_scalar(negmax[:, g:g + 1], negmax[:, g:g + 1], -MLA_SCALE, None,
                                    ALU.mult).then_inc(S["ss_neg"], 1)
                    dve.wait_ge(S["se_done"], g + 1)
                    link(v.reciprocal(rsum[:, g:g + 1], rsum[:, g:g + 1]))
                    v.tensor_scalar(psm, psm, rsum[:, g:g + 1], None, ALU.mult).then_inc(S["ps_scaled"], 1)
                    if g == 1:
                        dve.wait_ge(S["cc_hi"], 1)
                        lo(cache_s[1][:, 0], craws[:, 0], cache_s[0][:, 0], "cc_lo")
                    dve.wait_ge(S["spt_hi"], g + 1)
                    lo(pT_s[:, 1, :, g * P:(g + 1) * P], s_view.rearrange("p (b q) -> p b q", q=P),
                       pT_s[:, 0, :, g * P:(g + 1) * P], "spt_lo")
                dve.wait_ge(S["ols_hi"], 1)
                lo(ol_s[:, 1], ps[:, OB, 0:2 * P], ol_s[:, 0], "ols_lo")
                dve.wait_ge(S["act_read"], aread(("uvs", 0)))
                z = ps[:, 2 * (AT[("uvs", 0)] % 2)]
                for r in range(2):
                    lo(o_ml[64 * r:64 * r + 64, 1, :, SEQ:T],
                       z[64 * r:64 * r + 64, 0:MH * DEC]
                       .rearrange("p (t c) -> p t c", t=PAIRS)[:, :, DEC * r:DEC * r + DEC],
                       o_ml[64 * r:64 * r + 64, 0, :, SEQ:T], "dve_read" if r else None)

                for j in range(KT):
                    for n, (t, g) in enumerate(((("ya", j), ("ga", j)), (("yb", j), ("gb", j)))):
                        dve.wait_ge(S["act_read"], aread(g))
                        if j == 0 or (j, n) == (1, 0):
                            dve.wait_ge(S["sig0"], 2 * j + n + 1)
                        dve.wait_ge(S["p_done"], AT[t] + 1)
                        if n == 0 and j > 0:
                            dve.wait_ge(S["mi_lo"], j)
                        v.tensor_tensor(halves(tmp[n]), ptile(AT[t]), halves(mix[:, 2 * n + j % 2, 0:T]),
                                        ALU.mult).then_inc(S["dve_read"], 1)
                    dve.wait_ge(S["dve_read"], dread(("yb", j)))
                    v.tensor_tensor(tmp[0], tmp[0], tmp[1], ALU.add).then_inc(S["mi_raw"], 1)
                    dve.wait_ge(S["mi_hi"], j + 1)
                    lo(mixin[:, 1, j], tmp[0], mixin[:, 0, j], "mi_lo")
                for j in range(KT):
                    add_squares(j, "act_read", aread(("out", j)))

                def residual(gain, which, n0, lows):
                    def low(j):
                        dve.wait_ge(S["xn_hi"], n0 + KT + j + 1)
                        lo(xn[:, 1, j], xT[:, j], xn[:, 0, j], "xn_lo")

                    dve.wait_ge(S["rstd_done"], which)
                    for j in range(0, KT, 2):
                        if j > 0:
                            dve.wait_ge(S["x_even"], (n0 + j) // 2)
                            dve.wait_ge(S["x_odd"], (n0 + j) // 2)
                        for i in (j, j + 1):
                            v.scalar_tensor_tensor(tmp[i % 2], fT[:, i], vv[:, gain + i:gain + i + 1], rstd[:],
                                                   ALU.mult, ALU.mult).then_inc(S["r_mul"], 1)
                        dve.wait_ge(S["r_mul"], n0 + j + 1)
                        v.tensor_tensor(xT[:, j], xT[:, j], tmp[0], ALU.add).then_inc(S["x_even"], 1)
                        if lows:
                            if j > 0:
                                low(j - 1)
                            low(j)
                    if lows:
                        low(KT - 1)

                dve.wait_ge(S["f_raw"], KT)
                residual(V_GQM, 2, 0, False)
                v.memset(mix[:, 0:2, 0:2], 0.0).then_inc(S["zeroed"], 1)
                normed(KT, V_GPF, 3)

                def taps(t):
                    w, j = t[0] == "upv", t[1]
                    f, n = j + FT * w, 2 * j + w
                    dve.wait_ge(S["conv0"], n + 1)
                    link(v.scalar_tensor_tensor(uc[w], uext[w][:, 1:T + 3], vv[:, V_CW + 2 * FT + f:V_CW + 2 * FT + f + 1],
                                                uc[w], ALU.mult, ALU.add))
                    v.scalar_tensor_tensor(uc[w], uext[w][:, 2:T + 4], vv[:, V_CW + 4 * FT + f:V_CW + 4 * FT + f + 1],
                                           uc[w], ALU.mult, ALU.add).then_inc(S["conv2"], 1)

                def g_low(part, j):
                    dve.wait_ge(S["g_hi"], j + 1)
                    lo(g_s[part % 2][:, 1, j - _F0[part]], gt, g_s[part % 2][:, 0, j - _F0[part]], "g_lo")

                for part in (0, 1, "d0", 2, "d1", "d2"):
                    if part in (0, 1, 2):
                        for j in range(_F0[part], _F0[part + 1]):
                            taps(("upg", j))
                            if j > _F0[part]:
                                g_low(part, j - 1)
                            taps(("upv", j))
                            dve.wait_ge(S["gelu_done"], j + 1)
                            dve.wait_ge(S["conv2"], 2 * j + 2)
                            v.tensor_tensor(gt[:, 0:SEQ], gel[:, 0:SEQ], uc[1][:, 0:SEQ], ALU.mult)
                            v.tensor_tensor(gt[:, SEQ:T], gel[:, SEQ + 2:T + 2], uc[1][:, SEQ + 2:T + 2],
                                            ALU.mult).then_inc(S["g_raw"], 1)
                        g_low(part, _F0[part + 1] - 1)
                    elif part != "d0":
                        i = int(part[1])
                        for j in range(KT):
                            t = ("down", i, j)
                            if i == 1:
                                dve.wait_ge(S["act_read"], aread(("down", 0, j)))
                            else:
                                dve.wait_ge(S["dve_read"], dread(("down", 1, j)))
                            dve.wait_ge(S["p_done"], AT[t] + 1)
                            v.tensor_tensor(halves(fT[:, j]), ptile(AT[t]), halves(fT[:, j]), ALU.add).then_inc(S["dve_read"], 1)
                            if i == 2 and j > 0:
                                add_squares(KT + j - 1, "sq_done", j)
                add_squares(2 * KT - 1, "sq_done", KT)
                for k in range(PLE // P):
                    dve.wait_ge(S["p_hi"], k + 1)
                    lo(p_s[:, 1, k], mix[:, k, 0:T], p_s[:, 0, k], "p_lo")
                residual(V_GQF, 4, KT, True)

                for j in range(KT):
                    dve.wait_ge(S["act_read"], aread(("pleg", j)))
                    dve.wait_ge(S["p_done"], AT[("plep", j)] + 1)
                    if j >= 2:
                        dve.wait_ge(S["x_new"], j - 1)
                    v.tensor_tensor(halves(tmp[j % 2]), ptile(AT[("plep", j)]), halves(mix[:, j % 2, 0:T]),
                                    ALU.mult).then_inc(S["dve_read"], 1)
                    dve.wait_ge(S["dve_read"], dread(("plep", j)))
                    v.tensor_tensor(xT[:, j], xT[:, j], tmp[j % 2], ALU.add).then_inc(S["x_new"], 1)
                    if j >= 2:
                        add_squares(2 * KT + j - 2, "sq_done", KT + j - 1)
                for j in (KT - 2, KT - 1):
                    add_squares(2 * KT + j, "sq_done", KT + j + 1)

            @block.tensor
            def _(pe):
                PARTS = ((0, 0), (0, 1), (1, 0))

                def banks_free(t):
                    n = AT[t]
                    if n >= 2:
                        if act_upto[n - 1]:
                            pe.wait_ge(S["act_read"], act_upto[n - 1])
                        if dve_upto[n - 1]:
                            pe.wait_ge(S["dve_read"], dve_upto[n - 1])

                def project(t, chunk, rhs, nk, k0=0, ready=None, ks=None):
                    ks = range(nk) if ks is None else ks
                    if ks[0] == 0:
                        banks_free(t)
                        pe.wait_ge(S["w_lo"], CHUNK_AT[chunk] + 1)
                    w = wsp[:, RING_AT[chunk] % W_SLOTS]
                    z = ptile(AT[t])
                    for k in ks:
                        if ready is not None:
                            pe.wait_ge(S[ready[0]], ready[1] + k + 1)
                        for x, y in PARTS:
                            for h in range(2):
                                mm = pe.matmul(z[:, h], w[:, x, (k0 + k) * P:(k0 + k + 1) * P],
                                               rhs[:, y, k, h * HT:(h + 1) * HT],
                                               start=(k == 0 and (x, y) == (0, 0)), stop=(k == nk - 1 and x == 1))
                    if ks[-1] == nk - 1:
                        mm.then_inc(S["p_done"], 1)

                def half(t, i):
                    project(t, t, xn, KT, ks=range(i * KT // 2, (i + 1) * KT // 2))

                def sums(t, src):
                    banks_free(t)
                    z = ptile(AT[t])
                    for h in range(2):
                        mm = pe.matmul(z[:, h], ones, src[:, h * HT:(h + 1) * HT], start=True, stop=True)
                    mm.then_inc(S["p_done"], 1)

                for c in range(4):
                    pe.wait_ge(S["w_lo"], c + 1)
                    w = wsp[:, RING_AT[("v", c)] % W_SLOTS]
                    for k in range(2 * c, 2 * c + 2):
                        pe.wait_ge(S["xn_lo"], k + 1)
                        for i in range(QB + 1):
                            cols = slice(i * P, (i + 1) * P) if i < QB else slice(TAIL, T)
                            for x, y in PARTS:
                                mm = pe.matmul(ps[:, 3 + i], xn[:, x, k, cols], w[:, y, (k % 2) * 512:(k % 2 + 1) * 512],
                                               start=(k == 0 and (x, y) == (0, 0)), stop=(k == KT - 1 and x == 1))
                    mm.then_inc(S["v_chunk"], 1)
                project(("q", 0), ("q", 0), xn, KT)
                pe.wait_ge(S["v_lo"], 1)
                project(("k", 0), ("k", 0), xn, KT)
                pe.wait_ge(S["v_lo"], QB + 1)

                def sb_scores(n):
                    u = units[n]
                    z, w = ps[:, ZB + n % 3], width(u)
                    if n >= 3:
                        pe.wait_ge(S["a_raw"], n - 2)
                    if u[0] == "p":
                        _, h, kb = u
                        t, r = h // 2, 64 * (h % 2)
                        if h % 2 == 0 and kb == QB - 1:
                            pe.wait_ge(S["dve_read"], dread(("k", t)))
                        for i, (x, y) in enumerate(PARTS):
                            mm = pe.matmul(z[:, 0:w], qk[r:r + 64, t % 2, 1, x, kb * P:(kb + 1) * P],
                                           qk[r:r + 64, t % 2, 0, y, kb * P:SEQ], start=(i == 0), stop=False,
                                           skip_group_check=True)
                        mm = pe.matmul(z[:, 0:P], ident_b, masks[:, 1], start=False, stop=True, skip_group_check=True)
                    else:
                        kb = u[2]
                        if kb < CB:
                            pe.wait_ge(S["kc_lo"], CB - kb)
                        for t in range(PAIRS):
                            for i, (x, y) in enumerate(PARTS):
                                k = k_tail[:, x, t] if kb == CB else kcs[:, x, (CB - 1 - kb) % 2, t * P:(t + 1) * P]
                                mm = pe.matmul(z[:, 64 * t:64 * t + 64], k, q_smp[:, y, t],
                                               start=(t == 0 and i == 0), stop=(i == 2 and t == PAIRS - 1),
                                               skip_group_check=True)
                        if kb == CB:
                            mm = pe.matmul(z[:, 0:2 * P], ident_b, masks[:, 2:4], start=False, stop=True,
                                           skip_group_check=True)
                    mm.then_inc(S["z_done"], 1)

                def sb_sums(n):
                    u = units[n]
                    z, w = ps[:, ZB + n % 3], width(u)
                    pe.wait_ge(S["sp_lo"], n + 1)
                    first = n - (QB - 1 - u[2]) if u[0] == "p" else NPU
                    for x in range(2):
                        for m in range(first, n):
                            o, w2 = sp_off(units[m]), width(units[m])
                            pe.matmul(z[:, w - w2:w], exact[:, 1], sp[:, x, o:o + w2], start=False, stop=False,
                                      skip_group_check=True)
                        mm = pe.matmul(z[:, 0:w], exact[:, 0], sp[:, x, sp_off(u):sp_off(u) + w],
                                       start=False, stop=(x == 1), skip_group_check=True)
                    mm.then_inc(S["cum_done"], 1)

                def sb_pv(n):
                    u = units[n]
                    w = width(u)
                    pe.wait_ge(S["a_lo"], n + 1)
                    if u[0] == "p":
                        _, h, kb = u
                        if kb == QB - 1 and h > 0:
                            pe.wait_ge(S["o_lo"], h)
                        t = h // 2
                        for i, (x, y) in enumerate(PARTS):
                            mm = pe.matmul(ps[:, OB, SEQ - w:SEQ], v_s[:, x, kb, t * P:(t + 1) * P], att[:, n % 2, y, 0:w],
                                           start=(kb == QB - 1 and i == 0), stop=(kb == 0 and i == 2), skip_group_check=True)
                    else:
                        kb = u[2]
                        if kb == CB:
                            pe.wait_ge(S["o_lo"], SH)
                        else:
                            pe.wait_ge(S["vc_lo"], CB - kb)
                        for t in range(PAIRS):
                            for i, (x, y) in enumerate(PARTS):
                                slot = QB if kb == CB else (CB - 1 - kb) % 4
                                mm = pe.matmul(ps[:, OB, 64 * t:64 * t + 64], v_s[:, x, slot, t * P:(t + 1) * P],
                                               att[:, n % 2, y, 64 * t:64 * t + 64],
                                               start=(kb == CB and t == 0 and i == 0),
                                               stop=(kb == 0 and t == PAIRS - 1 and i == 2), skip_group_check=True)
                    mm.then_inc(S["pv_done"], 1)

                for s in range(NSTEP - 1):
                    if s < NU:
                        sb_scores(s)
                    if 0 <= s - LAG_CUM < NU:
                        sb_sums(s - LAG_CUM)
                    if 0 <= s - LAG_PV < NU:
                        sb_pv(s - LAG_PV)
                    for t, i in fill.get(s, []):
                        half(t, i)
                    if s == CN_STEP:
                        pe.wait_ge(S["act_read"], aread(("c", 0)))
                        sums(("cn", 0), sq[0])

                pe.wait_ge(S["c_ready"], 1)
                banks_free(("ct", 0))
                n = AT[("ct", 0)]
                for i in range(QB + 1):
                    cols = slice(i * P, (i + 1) * P) if i < QB else slice(TAIL, T)
                    mm = pe.transpose(ps[:, 2 * (n % 2) + i // QB, (i % QB) * P:(i % QB + 1) * P], craw[:, cols], ident)
                mm.then_inc(S["p_done"], 1)

                def m_tile(t):
                    banks_free(t)
                    z, h = ps[:, 2 * (AT[t] % 2)], t[1]
                    r, p0 = 64 * (h % 2), h // 2 * P
                    if t[0] == "ql":
                        pe.wait_ge(S["w_lo"], CHUNK_AT[("ukuv", 0)] + 1)
                        pe.wait_ge(S["dve_read"], dread(("qn", h // 2)))
                        for i, (x, y) in enumerate(PARTS):
                            pe.matmul(z, ukuv[r:r + 64, x, p0:p0 + P], qn[r:r + 64, y, 0:SEQ], start=(i == 0), stop=(i == 2))
                        for i, (x, y) in enumerate(PARTS):
                            mm = pe.matmul(ps[:, 2 * (AT[t] % 2) + 1, 0:DEC], ukuv[r:r + 64, x, p0:p0 + P],
                                           qn[r:r + 64, y, SEQ:T], start=(i == 0), stop=(i == 2))
                    elif t[0] == "ol":
                        pe.wait_ge(S["pt_lo"], QB * (h + 1))
                        for kb in range(QB):
                            o = kb * PTS
                            for x, y in PARTS:
                                mm = pe.matmul(z[:, kb * P:SEQ], ctok[:, x, kb], pT[:, y, o + kb * P:o + SEQ],
                                               start=(kb == 0 and (x, y) == (0, 0)), stop=(kb == QB - 1 and x == 1))
                    else:
                        pe.wait_ge(S["dve_read"], dread(("ol", h)))
                        for i, (x, y) in enumerate(PARTS):
                            mm = pe.matmul(z, ukuv[:, x, 512 + p0:512 + p0 + P], ol[:, y], start=(i == 0), stop=(i == 2))
                    mm.then_inc(S["p_done"], 1)

                m_tile(("ql", 0))
                for s in range(M_STEPS):
                    n = s - 2
                    if 0 <= n < NM:
                        h, qb = m_units[n]
                        pe.wait_ge(S["p_scaled"], n + 1)
                        if n >= 2:
                            pe.wait_ge(S["pt_lo"], n - 1)
                        for kb in range(qb + 1):
                            mm = pe.transpose(ps[:, TB + n % 2, kb * P:(kb + 1) * P], prw[:, n % 2, kb * P:(kb + 1) * P], ident)
                        mm.then_inc(S["tr_done"], 1)
                    if s < NM:
                        h, qb = m_units[s]
                        a, g, w = 32 * (h % 4), h // 4, P * (qb + 1)
                        z = ps[:, ZB + s % 2, 0:w]
                        pe.wait_ge(S["dve_read"], dread(("ql", h)))
                        if s == 0:
                            pe.wait_ge(S["rope_lo"], 3)
                            pe.wait_ge(S["c_lo"], 1)
                        if s >= 2:
                            pe.wait_ge(S["e_done"], s - 1)
                        for i, (x, y) in enumerate(PARTS):
                            pe.matmul(z, ql[:, x, qb * P:(qb + 1) * P], cT[:, y, 0:w], start=(i == 0), stop=False,
                                      skip_group_check=True)
                        for i, (x, y) in enumerate(PARTS):
                            pe.matmul(z, qr[a:a + 32, x, g, qb * P:(qb + 1) * P], krT[a:a + 32, y, 0:w], start=False, stop=False,
                                      tile_position=(a, 0), skip_group_check=True)
                        pe.matmul(z[:, qb * P:w], ident_b, masks[:, 4], start=False, stop=True,
                                  skip_group_check=True).then_inc(S["s_done"], 1)
                    for i, f in enumerate(QN_STEPS):
                        if s % (2 * QB) == f and s // (2 * QB) + 1 < PAIRS:
                            half(("qn", s // (2 * QB) + 1), i)
                    if s in GA_STEPS:
                        half(("ga", 0), GA_STEPS.index(s))
                    for t in m_tiles(s):
                        if t[0] not in ("qn", "ga"):
                            m_tile(t)

                for g in range(2):
                    if g > 0:
                        pe.wait_ge(S["spt_lo"], g)
                    else:
                        half(("gb", 0), 0)
                        pe.wait_ge(S["cs_lo"], 1)
                    for c in range(3):
                        z = ps[:, ZB + c] if c < 2 else ps[:, ZB + 2, 0:P]
                        ck = [(cache_s[y][:, 0, c * 512:(c + 1) * 512] if c < 2 else cT[:, y, TAIL:T]) for y in range(2)]
                        rk = [(cache_s[y][:, 1, c * 512:(c + 1) * 512] if c < 2 else krT[:, y, TAIL:T]) for y in range(2)]
                        for i, (x, y) in enumerate(PARTS):
                            pe.matmul(z, ql_smp[:, x, 4 * g:4 * g + 4], ck[y], start=(i == 0), stop=False)
                        for i, (x, y) in enumerate(PARTS):
                            mm = pe.matmul(z, qr_smp[:, x, g], rk[y], start=False, stop=(i == 2 and c < 2))
                        if c == 2:
                            mm = pe.matmul(z, ident_b, masks[:, 5], start=False, stop=True)
                    mm.then_inc(S["ss_done"], 1)
                    half((("gb", 0), ("ga", 1))[g], 1)
                    pe.wait_ge(S["ps_scaled"], g + 1)
                    for kb in range(CB + 1):
                        mm = pe.transpose(ps[:, ZB + kb // 4, (kb % 4) * P:(kb % 4 + 1) * P], psm[:, kb * P:(kb + 1) * P], ident)
                    mm.then_inc(S["str_done"], 1)
                    half((("ga", 1), ("gb", 1))[g], 0)
                pe.wait_ge(S["spt_lo"], 2)
                pe.wait_ge(S["cc_lo"], 1)
                for kb in range(CB + 1):
                    for x, y in PARTS:
                        c = cache_s[x][:, 0, kb * P:(kb + 1) * P] if kb < CB else ctok[:, x, QB]
                        mm = pe.matmul(ps[:, OB, 0:2 * P], c, pT_s[:, y, kb], start=(kb == 0 and (x, y) == (0, 0)),
                                       stop=(kb == CB and x == 1))
                mm.then_inc(S["ols_mm"], 1)
                half(("gb", 1), 1)
                banks_free(("uvs", 0))
                pe.wait_ge(S["ols_lo"], 1)
                for t in range(PAIRS):
                    for i, (x, y) in enumerate(PARTS):
                        mm = pe.matmul(ps[:, 2 * (AT[("uvs", 0)] % 2), 64 * t:64 * t + 64],
                                       ukuv[:, x, 512 + t * P:512 + (t + 1) * P], ol_s[:, y, 64 * t:64 * t + 64],
                                       start=(i == 0), stop=(i == 2))
                mm.then_inc(S["p_done"], 1)

                for j in range(KT):
                    project(("ya", j), ("proj", j), o_sb, PAIRS)
                    if j == 0:
                        pe.wait_ge(S["dve_read"], dread(("uvs", 0)))
                    project(("yb", j), ("proj", j), o_ml, PAIRS, PAIRS)
                    if j + 2 < KT:
                        project(("ga", j + 2), ("ga", j + 2), xn, KT)
                        project(("gb", j + 2), ("gb", j + 2), xn, KT)
                for j in range(KT):
                    project(("out", j), ("out", j), mixin, KT, ready=("mi_lo", 0) if j == 0 else None)
                pe.wait_ge(S["acc_done"], KT)
                sums(("nm", 1), acc)
                banks_free(("nm", 2))
                z = ptile(AT[("nm", 2)])
                for j in range(KT):
                    pe.wait_ge(S["sq2_done"], j + 1)
                    for h in range(2):
                        mm = pe.matmul(z[:, h], ones, sq[j % 2][:, h * HT:(h + 1) * HT], start=(j == 0), stop=(j == KT - 1))
                    mm.then_inc(S["sq2_sum" if j < KT - 1 else "p_done"], 1)

                for part in (0, 1, "d0", 2, "d1", "d2"):
                    if part in (0, 1, 2):
                        for t in _up(part):
                            project(t, t, xn, KT, ready=("xn_lo", KT) if t == ("upg", 0) else None)
                    else:
                        i = int(part[1])
                        for j in range(KT):
                            project(("down", i, j), ("down", i, j), g_s[i % 2], FFN_PARTS[i],
                                    ready=("g_lo", _F0[i]) if j == 0 else None)
                pe.wait_ge(S["acc_done"], 2 * KT)
                sums(("nm", 3), acc)

                for j in range(KT):
                    project(("pleg", j), ("pleg", j), xn, KT, ready=("xn_lo", 2 * KT) if j == 0 else None)
                    if j == 0:
                        pe.wait_ge(S["p_lo"], PLE // P)
                    project(("plep", j), ("plep", j), p_s, PLE // P)
                pe.wait_ge(S["acc_done"], 3 * KT)
                sums(("nm", 0), acc)

            st.close()
            sems = list(S.values()) + raw_in
            for i, engine in enumerate((nc.gpsimd, nc.vector, nc.scalar, nc.sync)):
                for sem in sems[i::4]:
                    engine.sem_clear(sem)
            nc.all_engine_barrier()

        with ExitStack() as st:
            y_st = st.enter_context(nc.semaphore("y_st"))
            block = st.enter_context(nc.Block())

            @block.sync
            def _(sp_):
                sp_.dma_start(y_out.rearrange("(k p) t -> p k t", p=P), xT[:]).then_inc(y_st, 16)
                sp_.wait_ge(y_st, 16)


def _shape_constants():
    c = np.zeros((P, NCONST), np.float32)
    k, q = np.arange(P)[:, None], np.arange(P)[None, :]
    c[:, C_ONES:C_ONES + P] = 1.0
    c[:, C_ID:C_ID + P] = np.eye(P)
    c[:, C_TRI:C_TRI + P] = np.where(k >= q, -1.0, 0.0)
    c[:, C_NEG1:C_NEG1 + P] = -1.0
    c[:, C_MD:C_MD + P] = np.where(k < q, 0.0, NEG)
    new = k - (P - DEC)
    one = np.where((new >= 0) & (new < np.arange(DEC)[None, :]), 0.0, NEG)
    c[:, C_MS:C_MS + 2 * P] = np.tile(one, (1, SH))
    c[:, C_MM:C_MM + P] = np.where((q // CHUNK) <= (k // CHUNK), 0.0, NEG)
    c[:, C_MT:C_MT + P] = np.where(q >= P - DEC, 0.0, NEG) + 0.0 * k
    half = ROPE // 2
    freqs = np.power(np.float32(10000.0), -np.arange(half, dtype=np.float32) / np.float32(half)).astype(np.float32)
    pos = np.concatenate([np.arange(SEQ), PAST + np.arange(DEC)]).astype(np.float32)
    ang = (pos[None, :] * freqs[:, None]).astype(np.float32)
    cs, sn = np.cos(ang), np.sin(ang)
    trig = np.concatenate([np.tile(np.concatenate([cs, cs]), (4, 1)),
                           np.tile(np.concatenate([-sn, sn]), (4, 1))], axis=1).astype(np.float32)
    return c, trig


def _stream(w):
    win = w["w_in"]
    at = dict(zip(("q", "k", "v", "m", "c", "r", "ga", "gb"),
                  np.cumsum([0, 512, 512, 512, MH * (NOPE + ROPE), LORA, ROPE, D]).tolist()))
    m = win[:, at["m"]:at["c"]].reshape(D, MH, NOPE + ROPE)

    def tiles(cols):
        nk = cols.shape[0] // P
        return cols.reshape(nk, P, -1).transpose(1, 0, 2).reshape(P, -1)

    out = np.zeros((len(CHUNKS), P, CW), np.float32)
    for n, c in enumerate(CHUNKS):
        kind, i = c[0], c[1]
        if kind == "v":
            a = tiles(win[2 * i * P:2 * (i + 1) * P, at["v"]:at["v"] + 512])
        elif kind in ("q", "k", "ga", "gb"):
            a = tiles(win[:, at[kind] + i * P:at[kind] + (i + 1) * P])
        elif kind == "c":
            a = tiles(win[:, at["c"]:at["r"]])
        elif kind == "kr":
            a = tiles(np.tile(win[:, at["r"]:at["ga"]], (1, 4)))
        elif kind == "qr":
            a = tiles(m[:, 4 * i:4 * i + 4, NOPE:].reshape(D, P))
        elif kind == "qn":
            a = tiles(m[:, 2 * i:2 * i + 2, :NOPE].reshape(D, P))
        elif kind == "ukuv":
            uk = w["w_uk"].reshape(LORA, PAIRS, 2 * NOPE).transpose(2, 1, 0).reshape(P, PAIRS * LORA)
            a = np.concatenate([uk, w["w_uv"].reshape(LORA, MH * MV)], axis=1)
        elif kind == "proj":
            a = np.concatenate([tiles(w["w_proj_sb"][:, i * P:(i + 1) * P]),
                                tiles(w["w_proj_mla"][:, i * P:(i + 1) * P])], axis=1)
        elif kind == "out":
            a = tiles(w["w_out"][:, i * P:(i + 1) * P])
        elif kind in ("upg", "upv"):
            f = i + FT * (kind == "upv")
            a = tiles(w["w_up"][:, f * P:(f + 1) * P])
        elif kind == "down":
            j = c[2]
            a = tiles(w["w_down"][_F0[i] * P:_F0[i + 1] * P, j * P:(j + 1) * P])
        elif kind == "pleg":
            a = tiles(w["w_ple_gate"][:, i * P:(i + 1) * P])
        else:
            a = tiles(w["w_ple_proj"][:, i * P:(i + 1) * P])
        out[n, :, :a.shape[1]] = a
    return out


_W = ("w_in", "w_uk", "w_uv", "w_proj_sb", "w_proj_mla", "w_out", "w_up", "w_down", "w_ple_gate", "w_ple_proj")


def _feature_major(rows):
    return rows.reshape(-1, P).T


def kernel(**inputs):
    import concourse.bacc as bacc
    from concourse.bass_utils import run_bass_kernel_spmd

    a = {n: np.asarray(x) for n, x in inputs.items()}
    consts, trig = _shape_constants()
    vecs = []
    for l in range(DEPTH):
        state = a["state_ffn_conv"][l, 0].reshape(2, 2 * FT, P).transpose(2, 1, 0).reshape(P, -1)
        parts = [_feature_major(a[n][l]) for n in ("g_pre_mix", "g_post_mix", "g_pre_ffn", "g_post_ffn",
                                                    "conv_w", "conv_b", "ckv_gain")]
        vecs.append(np.concatenate(parts + [state, np.zeros((P, 1), np.float32)], axis=1))
    blocks = lambda x: x.reshape(DEPTH, CB, P, -1)
    kcache = blocks(a["cache_sb_k"]).reshape(DEPTH, CB, P, PAIRS, P).transpose(0, 1, 4, 3, 2)
    rk = a["cache_mla_krope"][:, 0].transpose(0, 2, 1)
    ins = {
        "x_in": np.concatenate([a["x_prompt"][0], a["x_sample"][0]]).T,
        "p_in": np.concatenate([a["p_prompt"][:, 0], a["p_sample"][:, 0]], axis=1).transpose(0, 2, 1),
        "wstream": np.stack([_stream({n: a[n][l] for n in _W}) for l in range(DEPTH)]),
        "vec": np.stack(vecs),
        "kc": kcache.reshape(DEPTH, CB, P, PAIRS * P),
        "vc": blocks(a["cache_sb_v"]),
        "cct": a["cache_mla_ckv"][:, 0].transpose(0, 2, 1),
        "cc": a["cache_mla_ckv"][:, 0].reshape(DEPTH, CB, P, LORA).transpose(0, 2, 1, 3).reshape(DEPTH, P, CB * LORA),
        "krc": np.tile(rk, (1, 4, 1)),
        "consts": consts,
        "trig": trig,
    }
    outs = {"y_out": (D, T), "k_out": (DEPTH, SH * SD, T), "v_out": (DEPTH, T, SH * SD), "c_out": (DEPTH, LORA, T),
            "kr_out": (DEPTH, ROPE, T), "conv_out": (DEPTH, P, 2 * FT, 4)}
    nc = bacc.Bacc("TRN2", target_bir_lowering=False, num_devices=1, dynamic_dma_scratch_size=1024)
    arrays, args = {}, []
    for name, x in ins.items():
        x = np.ascontiguousarray(x)
        arrays[f"in_{name}"] = x
        args.append(nc.dram_tensor(f"in_{name}", x.shape, mybir.dt.from_np(x.dtype), kind="ExternalInput").ap())
    for name, shape in outs.items():
        args.append(nc.dram_tensor(f"out_{name}", shape, F32, kind="ExternalOutput").ap())
    build(nc, *args)
    r = run_bass_kernel_spmd(nc, [arrays], core_ids=[0]).results[0]
    y = r["out_y_out"].T
    k = r["out_k_out"].transpose(0, 2, 1).reshape(DEPTH, 1, T, SH, SD)
    v = r["out_v_out"].reshape(DEPTH, 1, T, SH, SD)
    c = r["out_c_out"].transpose(0, 2, 1)[:, None]
    kr = r["out_kr_out"].transpose(0, 2, 1)[:, None]
    cv = r["out_conv_out"].transpose(0, 3, 2, 1).reshape(DEPTH, 1, 4, 2 * DFF)
    halves = []
    for lo, hi in ((0, SEQ), (SEQ, T)):
        halves.append([k[:, :, lo:hi], v[:, :, lo:hi], c[:, :, lo:hi], kr[:, :, lo:hi]])
    halves[0].append(cv[:, :, 0:2])
    halves[1].append(cv[:, :, 2:4])
    out = [y[None, 0:SEQ], y[None, SEQ:T]] + halves[0] + halves[1]
    return tuple(np.ascontiguousarray(x) for x in out)
```
